# Optimizing a Trainium2 kernel written in Bass

```python
import jax, jax.numpy as jnp
from jax import lax
import numpy as np

D_MODEL = 1024
BATCH = 1
SEQ = 1024
DEPTH = 1
DEC_BATCH = 8
DEC_SEQ = 8
PAST_LEN = 2048
PAGE_SIZE = 128

HEAD_DIM = 64
MLA_HEADS = 8
MLA_Q_RANK = 256
MLA_KV_RANK = 128
MLA_NOPE = 64
MLA_ROPE = 32
MLA_V = 64
DIL_HEADS = 8
DIL_PAIRS = ((128, 1), (512, 4), (2048, 16))
MAX_WINDOW = 2048
D_MIX = MLA_HEADS * MLA_V + DIL_HEADS * HEAD_DIM
IN_COLS = MLA_Q_RANK + MLA_KV_RANK + MLA_ROPE + 3 * DIL_HEADS * HEAD_DIM
D_FF = 2816
CONV_W = 3
ROPE_THETA = 10000.0
EPS = 1e-6
Q_BLOCK = 128
NEG = -1e30
MLA_SCALE = (MLA_NOPE + MLA_ROPE) ** -0.5
DIL_SCALE = HEAD_DIM ** -0.5

kernel_name = "hymba_mla_dilated_swa_convffn_step"

def _rmsnorm(x, g):
    xf = x.astype(jnp.float32)
    y = xf * lax.rsqrt(jnp.mean(xf * xf, axis=-1, keepdims=True) + EPS)
    return (y * g.astype(jnp.float32)).astype(x.dtype)

def _rope(x, pos):
    half = x.shape[-1] // 2
    inv = ROPE_THETA ** (-jnp.arange(half, dtype=jnp.float32) / half)
    ang = pos.astype(jnp.float32)[:, None] * inv[None, :]
    cos = jnp.cos(ang)[:, None, :]
    sin = jnp.sin(ang)[:, None, :]
    xf = x.astype(jnp.float32)
    x1, x2 = xf[..., :half], xf[..., half:]
    return jnp.concatenate([x1 * cos - x2 * sin, x2 * cos + x1 * sin], axis=-1).astype(x.dtype)

def _softmax_lse(s):
    m = jnp.max(s, axis=-1, keepdims=True)
    e = jnp.exp(s - m)
    den = jnp.sum(e, axis=-1, keepdims=True)
    return e / den, (m + jnp.log(den))[..., 0]

def _project(xn, pos, w_in, g_q_a, w_q_b, g_kv_a):
    B, S, _ = xn.shape
    z = xn @ w_in
    o1 = MLA_Q_RANK
    o2 = o1 + MLA_KV_RANK
    o3 = o2 + MLA_ROPE
    dw = DIL_HEADS * HEAD_DIM
    cq = _rmsnorm(z[..., :o1], g_q_a)
    q = (cq @ w_q_b).reshape(B, S, MLA_HEADS, MLA_NOPE + MLA_ROPE)
    q_nope = q[..., :MLA_NOPE]
    q_rope = _rope(q[..., MLA_NOPE:], pos)
    ckv = _rmsnorm(z[..., o1:o2], g_kv_a)
    kr = _rope(z[..., o2:o3][:, :, None, :], pos)[:, :, 0, :]
    dq = _rope(z[..., o3:o3 + dw].reshape(B, S, DIL_HEADS, HEAD_DIM), pos)
    dk = _rope(z[..., o3 + dw:o3 + 2 * dw].reshape(B, S, DIL_HEADS, HEAD_DIM), pos)
    dv = z[..., o3 + 2 * dw:].reshape(B, S, DIL_HEADS, HEAD_DIM)
    return q_nope, q_rope, ckv, kr, dq, dk, dv

def _mla_prompt(q_nope, q_rope, ckv, kr, w_uk, w_uv):
    B, S, H, _ = q_nope.shape
    k_nope = jnp.einsum("bsc,chd->bshd", ckv, w_uk.reshape(MLA_KV_RANK, H, MLA_NOPE))
    v = jnp.einsum("bsc,chd->bshd", ckv, w_uv.reshape(MLA_KV_RANK, H, MLA_V))
    nb = S // Q_BLOCK
    qn = q_nope.reshape(B, nb, Q_BLOCK, H, MLA_NOPE).transpose(1, 0, 2, 3, 4)
    qr = q_rope.reshape(B, nb, Q_BLOCK, H, MLA_ROPE).transpose(1, 0, 2, 3, 4)
    kpos = jnp.arange(S)

    def block(args):
        qn_b, qr_b, j = args
        s = (jnp.einsum("bqhd,bkhd->bhqk", qn_b, k_nope)
             + jnp.einsum("bqhr,bkr->bhqk", qr_b, kr)).astype(jnp.float32) * MLA_SCALE
        qpos = j * Q_BLOCK + jnp.arange(Q_BLOCK)
        s = jnp.where(kpos[None, :] <= qpos[:, None], s, NEG)
        p = jax.nn.softmax(s, axis=-1)
        return jnp.einsum("bhqk,bkhd->bqhd", p.astype(v.dtype), v)

    o = lax.map(block, (qn, qr, jnp.arange(nb)))
    return o.transpose(1, 0, 2, 3, 4).reshape(B, S, H * MLA_V)

def _mla_sample(q_nope, q_rope, ckv, kr, cache_ckv, cache_kr, page_table, w_uk, w_uv):
    DB, T, H, _ = q_nope.shape
    past_c = cache_ckv[page_table].reshape(DB, -1, MLA_KV_RANK)
    past_r = cache_kr[page_table].reshape(DB, -1, MLA_ROPE)
    P = past_c.shape[1]
    c_all = jnp.concatenate([past_c, ckv], axis=1)
    r_all = jnp.concatenate([past_r, kr], axis=1)
    q_lat = jnp.einsum("bthd,chd->bthc", q_nope, w_uk.reshape(MLA_KV_RANK, H, MLA_NOPE))
    s = (jnp.einsum("bthc,bsc->bhts", q_lat, c_all)
         + jnp.einsum("bthr,bsr->bhts", q_rope, r_all)).astype(jnp.float32) * MLA_SCALE
    mask = jnp.arange(P + T)[None, :] <= (P + jnp.arange(T))[:, None]
    p = jax.nn.softmax(jnp.where(mask, s, NEG), axis=-1)
    o_lat = jnp.einsum("bhts,bsc->bthc", p.astype(c_all.dtype), c_all)
    o = jnp.einsum("bthc,chd->bthd", o_lat, w_uv.reshape(MLA_KV_RANK, H, MLA_V))
    return o.reshape(DB, T, H * MLA_V)

def _dil_branch_prompt(q, k, v, window, dil):
    B, S, H, Dh = q.shape
    L = S // dil
    blk = window // dil
    nb = -(-L // blk)
    Lp = nb * blk
    N = B * dil

    def sub(a):
        return a.reshape(B, L, dil, H, Dh).transpose(0, 2, 1, 3, 4).reshape(N, L, H, Dh)

    qs = jnp.pad(sub(q), ((0, 0), (0, Lp - L), (0, 0), (0, 0))).reshape(N, nb, blk, H, Dh)
    kp = jnp.pad(sub(k), ((0, 0), (blk, Lp - L), (0, 0), (0, 0))).reshape(N, nb + 1, blk, H, Dh)
    vp = jnp.pad(sub(v), ((0, 0), (blk, Lp - L), (0, 0), (0, 0))).reshape(N, nb + 1, blk, H, Dh)
    kb = jnp.concatenate([kp[:, :-1], kp[:, 1:]], axis=2)
    vb = jnp.concatenate([vp[:, :-1], vp[:, 1:]], axis=2)
    s = jnp.einsum("nbqhd,nbkhd->nbhqk", qs, kb).astype(jnp.float32) * DIL_SCALE
    qi = jnp.arange(blk)[:, None] + blk
    ki = jnp.arange(2 * blk)[None, :]
    dist = qi - ki
    kpos = jnp.arange(nb)[:, None, None] * blk + ki[None] - blk
    valid = (dist >= 0) & (dist <= blk) & (kpos >= 0)
    p, lse = _softmax_lse(jnp.where(valid[None, :, None], s, NEG))
    o = jnp.einsum("nbhqk,nbkhd->nbqhd", p.astype(vb.dtype), vb)
    o = o.reshape(B, dil, Lp, H, Dh)[:, :, :L].transpose(0, 2, 1, 3, 4).reshape(B, S, H, Dh)
    lse = lse.transpose(0, 1, 3, 2).reshape(B, dil, Lp, H)[:, :, :L].transpose(0, 2, 1, 3).reshape(B, S, H)
    return o, lse

def _combine_dil(outs, lses):
    wts = jax.nn.softmax(jnp.stack(lses, axis=0), axis=0)
    o = jnp.einsum("gbsh,gbshd->bshd", wts.astype(outs[0].dtype), jnp.stack(outs, axis=0))
    return o.reshape(o.shape[0], o.shape[1], -1)

def _dil_prompt(q, k, v):
    outs, lses = [], []
    for window, dil in DIL_PAIRS:
        o, lse = _dil_branch_prompt(q, k, v, window, dil)
        outs.append(o)
        lses.append(lse)
    return _combine_dil(outs, lses)

def _dil_sample(q, k, v, win_k, win_v):
    DB, T, H, Dh = q.shape
    Wb = win_k.shape[1]
    k_all = jnp.concatenate([win_k, k], axis=1)
    v_all = jnp.concatenate([win_v, v], axis=1)
    outs, lses = [], []
    for window, dil in DIL_PAIRS:
        nk = window // dil + 1
        idx = Wb + jnp.arange(T)[:, None] - dil * jnp.arange(nk)[None, :]
        valid = idx >= 0
        idx_c = jnp.maximum(idx, 0)
        kg = k_all[:, idx_c]
        vg = v_all[:, idx_c]
        s = jnp.einsum("bthd,btkhd->bthk", q, kg).astype(jnp.float32) * DIL_SCALE
        p, lse = _softmax_lse(jnp.where(valid[None, :, None, :], s, NEG))
        outs.append(jnp.einsum("bthk,btkhd->bthd", p.astype(vg.dtype), vg))
        lses.append(lse)
    return _combine_dil(outs, lses)

def _conv_ffn(xn, conv_state, w_gate, w_up, conv_w, conv_b, w_down):
    T = xn.shape[1]
    g = xn @ w_gate
    u = xn @ w_up
    gp = jnp.concatenate([conv_state, g], axis=1)
    gc = conv_b + sum(conv_w[j] * gp[:, j:j + T] for j in range(CONV_W))
    y = (jax.nn.silu(gc) * u) @ w_down
    return y, gp[:, -(CONV_W - 1):]

def _block(x, pos, conv_state, mla_fn, dil_fn, g_attn, w_in, g_q_a, w_q_b, g_kv_a, w_out,
           g_ffn, w_gate, w_up, conv_w, conv_b, w_down):
    xn = _rmsnorm(x, g_attn)
    q_nope, q_rope, ckv, kr, dq, dk, dv = _project(xn, pos, w_in, g_q_a, w_q_b, g_kv_a)
    o = jnp.concatenate([mla_fn(q_nope, q_rope, ckv, kr), dil_fn(dq, dk, dv)], axis=-1)
    h = x + o @ w_out
    y, conv_new = _conv_ffn(_rmsnorm(h, g_ffn), conv_state, w_gate, w_up, conv_w, conv_b, w_down)
    return h + y, ckv, kr, dk, dv, conv_new

def setup_inputs(seed: int = 0) -> dict:
    key = jax.random.key(seed)
    ks = jax.random.split(key, 32)
    f32 = jnp.float32

    def nrm(k, shape, scale):
        return jax.random.normal(k, shape, f32) * scale

    def gain(k, shape):
        return 1.0 + 0.05 * jax.random.normal(k, shape, f32)

    n_pages = PAST_LEN // PAGE_SIZE
    n_pool = (DEC_BATCH * n_pages * 5) // 4
    w_buf = min(MAX_WINDOW, PAST_LEN)
    page_table = jax.random.permutation(ks[0], n_pool)[:DEC_BATCH * n_pages].reshape(DEC_BATCH, n_pages).astype(jnp.int32)
    return {
        "x_prompt": nrm(ks[1], (BATCH, SEQ, D_MODEL), 1.0),
        "x_sample": nrm(ks[2], (DEC_BATCH, DEC_SEQ, D_MODEL), 1.0),
        "cache_kv_latent": nrm(ks[3], (DEPTH, n_pool, PAGE_SIZE, MLA_KV_RANK), 1.0),
        "cache_k_rope": nrm(ks[4], (DEPTH, n_pool, PAGE_SIZE, MLA_ROPE), 1.0),
        "state_win_k": nrm(ks[5], (DEPTH, DEC_BATCH, w_buf, DIL_HEADS, HEAD_DIM), 1.0),
        "state_win_v": nrm(ks[6], (DEPTH, DEC_BATCH, w_buf, DIL_HEADS, HEAD_DIM), 1.0),
        "state_ffn_conv": nrm(ks[7], (DEPTH, DEC_BATCH, CONV_W - 1, D_FF), 1.0),
        "page_table": page_table,
        "g_attn": gain(ks[8], (DEPTH, D_MODEL)),
        "w_in": nrm(ks[9], (DEPTH, D_MODEL, IN_COLS), D_MODEL ** -0.5),
        "g_q_a": gain(ks[10], (DEPTH, MLA_Q_RANK)),
        "w_q_b": nrm(ks[11], (DEPTH, MLA_Q_RANK, MLA_HEADS * (MLA_NOPE + MLA_ROPE)), MLA_Q_RANK ** -0.5),
        "g_kv_a": gain(ks[12], (DEPTH, MLA_KV_RANK)),
        "w_uk": nrm(ks[13], (DEPTH, MLA_KV_RANK, MLA_HEADS * MLA_NOPE), MLA_KV_RANK ** -0.5),
        "w_uv": nrm(ks[14], (DEPTH, MLA_KV_RANK, MLA_HEADS * MLA_V), MLA_KV_RANK ** -0.5),
        "w_out": nrm(ks[15], (DEPTH, D_MIX, D_MODEL), D_MIX ** -0.5),
        "g_ffn": gain(ks[16], (DEPTH, D_MODEL)),
        "w_gate": nrm(ks[17], (DEPTH, D_MODEL, D_FF), D_MODEL ** -0.5),
        "w_up": nrm(ks[18], (DEPTH, D_MODEL, D_FF), D_MODEL ** -0.5),
        "conv_w": nrm(ks[19], (DEPTH, CONV_W, D_FF), CONV_W ** -0.5),
        "conv_b": nrm(ks[20], (DEPTH, D_FF), 0.01),
        "w_down": nrm(ks[21], (DEPTH, D_FF, D_MODEL), D_FF ** -0.5),
        "g_final": gain(ks[22], (D_MODEL,)),
    }

def reference(x_prompt, x_sample, cache_kv_latent, cache_k_rope, state_win_k, state_win_v, state_ffn_conv,
              page_table, g_attn, w_in, g_q_a, w_q_b, g_kv_a, w_uk, w_uv, w_out, g_ffn, w_gate, w_up,
              conv_w, conv_b, w_down, g_final):
    B, S, _ = x_prompt.shape
    DB, T, _ = x_sample.shape
    past_len = page_table.shape[1] * cache_kv_latent.shape[2]
    w_prompt = min(MAX_WINDOW, S)
    w_buf = state_win_k.shape[2]
    pos_p = jnp.arange(S, dtype=jnp.int32)
    pos_s = past_len + jnp.arange(T, dtype=jnp.int32)
    conv_zero = jnp.zeros((B, CONV_W - 1, D_FF), x_prompt.dtype)

    xp, xs = x_prompt, x_sample
    p_ckv, p_kr, p_wk, p_wv, p_conv = [], [], [], [], []
    s_ckv, s_kr, s_wk, s_wv, s_conv = [], [], [], [], []
    for l in range(DEPTH):
        shared = (g_attn[l], w_in[l], g_q_a[l], w_q_b[l], g_kv_a[l], w_out[l],
                  g_ffn[l], w_gate[l], w_up[l], conv_w[l], conv_b[l], w_down[l])
        xp, ckv, kr, dk, dv, cnew = _block(
            xp, pos_p, conv_zero,
            lambda qn, qr, c, r: _mla_prompt(qn, qr, c, r, w_uk[l], w_uv[l]),
            _dil_prompt, *shared)
        p_ckv.append(ckv)
        p_kr.append(kr)
        p_wk.append(dk[:, -w_prompt:])
        p_wv.append(dv[:, -w_prompt:])
        p_conv.append(cnew)

        xs, ckv, kr, dk, dv, cnew = _block(
            xs, pos_s, state_ffn_conv[l],
            lambda qn, qr, c, r: _mla_sample(qn, qr, c, r, cache_kv_latent[l], cache_k_rope[l], page_table, w_uk[l], w_uv[l]),
            lambda q, k, v: _dil_sample(q, k, v, state_win_k[l], state_win_v[l]),
            *shared)
        s_ckv.append(ckv)
        s_kr.append(kr)
        s_wk.append(jnp.concatenate([state_win_k[l], dk], axis=1)[:, -w_buf:])
        s_wv.append(jnp.concatenate([state_win_v[l], dv], axis=1)[:, -w_buf:])
        s_conv.append(cnew)

    y_prompt = _rmsnorm(xp, g_final)
    y_sample = _rmsnorm(xs, g_final)
    return (y_prompt, y_sample,
            jnp.stack(p_ckv), jnp.stack(p_kr), jnp.stack(p_wk), jnp.stack(p_wv), jnp.stack(p_conv),
            jnp.stack(s_ckv), jnp.stack(s_kr), jnp.stack(s_wk), jnp.stack(s_wv), jnp.stack(s_conv))


_drawn_inputs = setup_inputs


def setup_inputs(seed=0):
    import zlib

    import numpy as np

    out = dict(_drawn_inputs(seed))
    spreads = {}
    factors = {'cache_k_rope': 3.695, 'g_q_a': 8.0, 'conv_b': 8.0}
    for name, (base, spread) in spreads.items():
        noise = np.random.default_rng([zlib.crc32(name.encode()), seed]).standard_normal(out[name].shape)
        drawn = base * np.exp(spread * noise) if base else spread * noise
        out[name] = __import__('jax').numpy.asarray(drawn.astype(out[name].dtype))
    for name, factor in factors.items():
        out[name] = (out[name] * factor).astype(out[name].dtype)
    return out
```

```python
import concourse.bass as bass
from concourse import mybir
from contextlib import ExitStack
import numpy as np

F32 = mybir.dt.float32
F32R = mybir.dt.float32r
I32 = mybir.dt.int32
ALU = mybir.AluOpType
ACT = mybir.ActivationFunctionType
AX = mybir.AxisListType

P = 128
D_MODEL = 1024
SEQ = 1024
DEC_B = 8
DEC_T = 8
PAST = 2048
PAGE = 128
HEADS = 8
HD = 64
Q_RANK = 256
KV_RANK = 128
NOPE = 64
ROPE = 32
QK = NOPE + ROPE
D_FF = 2816
CONV_W = 3
EPS = 1e-6
NEG = -1e30
HUGE = 3e38
MLA_SCALE = QK ** -0.5
DIL_SCALE = HD ** -0.5
DIL_PAIRS = ((128, 1), (512, 4), (2048, 16))
THETA = 10000.0

PT = SEQ // P
NT = PT + 1
NS = DEC_B * DEC_T
TOK = SEQ + NS
KC = D_MODEL // P
HW = HEADS * HD
PAGES = PAST // PAGE
PAIRS = HEADS // 2
FC = D_FF // P
G0 = Q_RANK + KV_RANK + ROPE
GROUPS = ((0, G0), (G0, HW), (G0 + HW, HW), (G0 + 2 * HW, HW))
IN_COLS = G0 + 3 * HW
RD, RM = HD // 2, ROPE // 2
ROT = 3 * RD + 3 * RM
FAR_ROWS = (PAST - 512) // 16
NEAR = 4
WIN_KEYS = DEC_T * FAR_ROWS + 512 + DEC_T


def full(t):
    return t[tuple(slice(None) for _ in t.shape)]


def shape_tables():
    f = np.float32
    pos = np.concatenate([np.arange(SEQ), np.tile(PAST + np.arange(DEC_T), DEC_B)]).astype(f)

    def angles(half):
        inv = f(THETA) ** (-np.arange(half, dtype=f) / f(half))
        a = (pos[:, None] * inv[None, :]).astype(f)
        return np.cos(a), np.sin(a)

    cd, sd = angles(RD)
    cm, sm = angles(RM)
    rot = np.concatenate([cd, cd, sd, cm, cm, sm], 1).astype(f)

    def times(d):
        return sum(((d >= 0) & (d <= w) & (d % r == 0)).astype(f) for w, r in DIL_PAIRS)

    def bias(d):
        c = times(d)
        return np.where(c > 0, np.log(np.maximum(c, 1)) / DIL_SCALE, NEG).astype(f)

    dist = np.arange(P)[:, None] + (SEQ - P) - np.arange(SEQ)[None, :]
    causal = np.where(dist >= 0, 0, NEG).astype(f)
    dilated = bias(dist)
    t = np.tile(np.arange(DEC_T), HEADS)[:, None]
    far = (16 * np.arange(FAR_ROWS)[None, :] + np.arange(DEC_T)[:, None]).reshape(-1)
    near = PAST - 512 + (np.arange(NEAR)[:, None] + NEAR * np.arange(P)[None, :]).reshape(-1)
    new = PAST + np.arange(DEC_T)
    window = bias(PAST + t - np.concatenate([far, new, near])[None, :])
    fresh = np.where(np.arange(DEC_T)[None, :] <= t, 0, NEG).astype(f)
    own = (np.arange(NS)[:, None] // DEC_T == np.arange(HW)[None, :] // HD).astype(f)
    return {
        "rot": rot, "causal": causal, "dilated": dilated, "window": window,
        "fresh": fresh, "own": own, "ident": np.eye(P, dtype=f),
    }


class Step:

    last = False

    def __init__(self, n, half, odd):
        self.n, self.half, self.odd = n, half, odd
        self.first = isinstance(n, int) and n == 0
        self.second = isinstance(n, int) and n == 1

    def after_next(self):
        return Step.of(self.n + 2) if isinstance(self.n, int) else Step(self.n + 2, self.half + 1, self.odd)

    @staticmethod
    def of(n):
        step = Step(n, n // 2, n % 2)
        if n:
            step.back = Step.of(n - 1)
        return step


def staged(eng, prep, main, count=NT, lead=None):
    turns = (count - 2) // 2
    if lead is None:
        prep(Step.of(0))
        prep(Step.of(1))
    else:
        lead()
    main(Step.of(0))
    with eng.Fori(0, turns) as it:
        for u in range(2):
            here = Step(it * 2 + (1 + u), it + u, (1 + u) % 2)
            ahead = Step(it * 2 + (2 + u), it + 1, u)
            ahead.back = here
            prep(ahead)
            main(here)
    for n in range(2 * turns + 1, count):
        here, ahead = Step.of(n), Step.of(n + 1)
        here.last = n == count - 1
        if not here.last:
            ahead.last = n + 1 == count - 1
            prep(ahead)
        main(here)


def project(nc, sem, io):
    ctx = ExitStack()
    with ctx:
        sb = lambda n, s, d=F32: ctx.enter_context(nc.sbuf_tensor(n, s, d))
        ps = lambda n, s: ctx.enter_context(nc.psum_tensor(n, s, F32))
        win_h = sb("win_h", [P, KC, IN_COLS], F32R)
        win_l = sb("win_l", [P, KC, IN_COLS], F32R)
        wqb_h = sb("wqb_h", [P, 2, HEADS * QK], F32R)
        wqb_l = sb("wqb_l", [P, 2, HEADS * QK], F32R)
        wkv_h = sb("wkv_h", [P, 2 * HW], F32R)
        wkv_l = sb("wkv_l", [P, 2 * HW], F32R)
        xT_h = [sb(f"xT_h{i}", [P, KC, P], F32R) for i in range(2)]
        xT_l = [sb(f"xT_l{i}", [P, KC, P], F32R) for i in range(2)]
        cT_h = sb("cT_h", [P, 3, P], F32R)
        cT_l = sb("cT_l", [P, 3, P], F32R)
        x = [sb(f"x{i}", [P, D_MODEL]) for i in range(2)]
        rot = [sb(f"rot{i}", [P, ROT]) for i in range(2)]
        xn = sb("xn", [P, D_MODEL])
        g_x = sb("g_x", [P, D_MODEL])
        g_c = sb("g_c", [P, Q_RANK + KV_RANK])
        ident = sb("ident1", [P, P])
        cn = sb("cn", [P, Q_RANK + KV_RANK])
        kr = sb("kr", [P, ROPE])
        krt = sb("krt", [P, 2, ROPE])
        qt = sb("qt", [P, 2, HEADS, ROPE])
        vm = sb("vm", [P, HW])
        work = sb("work", [P, 2, 4 * HW])
        dqk = work[:, 0, 0:2 * HW]
        rt = [work[:, 0, (2 + i) * HW:(3 + i) * HW] for i in range(2)]
        dv = work[:, 1, 0:HW]
        qm = work[:, 1, HW:HW + HEADS * QK]
        km = work[:, 1, HW + HEADS * QK:HW + 2 * HEADS * QK]
        st = sb("st1", [P, 10])
        xms, xrs, cms, crs, half, eps = (st[:, a:b] for a, b in ((0, 1), (1, 2), (2, 4), (4, 6), (6, 8), (8, 10)))
        zp = [ps(f"zp{g}", [P, 512]) for g in range(4)]
        xp = [ps(f"xp{i}", [P, 4, P]) for i in range(2)]
        cp = ps("cp", [P, 1024])
        S = {n: sem(n) for n in (
            "p_const wload0 wload1 wload2 wload3 xload0 xload1 rload0 rload1 w_hi w_lo p_half x_ms x_eps x_rs xn_ok xT_ps xT_hi xT_lo "
            "z0_ps z1_ps z2_ps z3_ps c_ms c_eps c_rs cn_ok cT_ps cT_hi cT_lo kr_a kr_ok d_a dq_ok dk_ok dv_ok "
            "q_ps q_nope q_a q_ok kv_ps k_nope k_rope v_ok "
            "o_c o_kr o_dq o_dk o_dv o_q o_k o_v sink").split()}
        wi = io["w_in"].rearrange("(k p) n -> p k n", p=P)
        loads = []
        for g, (c0, n) in enumerate(GROUPS):
            for k0 in range(0, KC, 2):
                loads.append((wi[:, k0:k0 + 2, c0:c0 + n], win_h[:, k0:k0 + 2, c0:c0 + n],
                              win_l[:, k0:k0 + 2, c0:c0 + n], (2, n)))
            if g == 1:
                for k in range(2):
                    loads.append((io["w_q_b"].rearrange("(k p) n -> p k n", p=P)[:, k:k + 1], wqb_h[:, k:k + 1],
                                  wqb_l[:, k:k + 1], (1, HEADS * QK)))
        for i, n in enumerate(("w_uk", "w_uv")):
            c = slice(i * HW, (i + 1) * HW)
            loads.append((io[n].unsqueeze(1), wkv_h[:, c], wkv_l[:, c], (1, HW)))
        ends = lambda t: isinstance(t.n, int) and t.n > NT - 3
        need = {0: 4, 1: 8, "q": 10, 2: 14, 3: 18, "kv": 20}
        SLOTS = 4
        slots = work[:].rearrange("p a b -> p (a b)").rearrange("p (s c) -> p s c", s=SLOTS)

        def slot(n):
            a, b = loads[n][3]
            return slots[:, n % SLOTS, 0:a * b].rearrange("p (a b) -> p a b", a=a)

        def flat(ap, n):
            return ap if len(ap.shape) == 3 else ap.rearrange("p (a b) -> p a b", a=loads[n][3][0])

        block = ctx.enter_context(nc.Block())

        @block.sync
        def _(sp):
            def load_x(t, src, rows=P):
                sp.dma_start(x[t.odd][0:rows, :], src).then_inc(S[f"xload{t.odd}"], 16)

            def load_rot(t, src, rows=P):
                sp.dma_start(rot[t.odd][0:rows, :], src).then_inc(S[f"rload{t.odd}"], 16)

            def load_w(n):
                if n >= SLOTS:
                    sp.wait_ge(S["w_lo"], n - SLOTS + 1)
                sp.dma_start(slot(n), loads[n][0]).then_inc(S[f"wload{n % SLOTS}"], 16)

            for n in (0, 1):
                load_x(Step.of(n), io["x_prompt"][n * P:(n + 1) * P, :])
                load_rot(Step.of(n), io["rot"][n * P:(n + 1) * P, :])
                if n == 0:
                    sp.dma_start(ident[:], io["ident"]).then_inc(S["p_const"], 16)
                    sp.dma_start(g_x[:], io["g_attn"].partition_broadcast(P)).then_inc(S["p_const"], 16)
                    sp.dma_start(g_c[:, 0:Q_RANK], io["g_q_a"].partition_broadcast(P)).then_inc(S["p_const"], 16)
                    sp.dma_start(g_c[:, Q_RANK:], io["g_kv_a"].partition_broadcast(P)).then_inc(S["p_const"], 16)
            for n in range(len(loads)):
                load_w(n)

            def store(t, ap, dst, ready, done, count=1):
                sp.wait_ge(S[ready], t.n * count + count)
                sp.dma_start(dst, ap).then_inc(S[done], 16)

            def stores(t):
                row = bass.ds(t.n * P, P)
                last = isinstance(t.n, int) and t.n == NT - 3
                if not (isinstance(t.n, int) and t.n > NT - 3):
                    sp.wait_ge(S["xn_ok"], t.n + 1)
                    if last:
                        load_x(t, io["x_sample"], NS)
                    else:
                        load_x(t, io["x_prompt"][bass.ds(t.n * P + 2 * P, P), :])
                store(t, kr[:], io["p_k_rope"][row, :], "kr_ok", "o_kr")
                store(t, cn[:, Q_RANK:], io["p_kv_latent"][row, :], "cn_ok", "o_c")
                store(t, dqk[:, 0:HW], io["s_dq"][row, :], "dq_ok", "o_dq")
                store(t, dqk[:, HW:], io["p_win_k"][row, :], "dk_ok", "o_dk")
                store(t, qm, io["s_q"][row, :], "q_ok", "o_q")
                if last:
                    load_rot(t, io["rot"][SEQ:TOK, :], NS)
                elif not (isinstance(t.n, int) and t.n > NT - 3):
                    load_rot(t, io["rot"][bass.ds(t.n * P + 2 * P, P), :])
                store(t, dv, io["p_win_v"][row, :], "dv_ok", "o_dv")
                sp.wait_ge(S["k_rope"], t.n + 1)
                store(t, km, io["s_k"][row, :], "k_nope", "o_k")
                store(t, vm[:], io["s_v"][row, :], "v_ok", "o_v")

            stores(Step.of(0))
            turns = (NT - 4) // 2
            with sp.Fori(0, turns) as it:
                for u in range(2):
                    stores(Step(it * 2 + (1 + u), it + u, (1 + u) % 2))
            for n in range(2 * turns + 1, NT - 1):
                stores(Step.of(n))
            t = Step.of(NT - 1)
            row = slice(SEQ, TOK)
            store(t, kr[0:NS, :], io["s_k_rope"], "kr_ok", "o_kr")
            store(t, cn[0:NS, Q_RANK:], io["s_kv_latent"], "cn_ok", "o_c")
            store(t, dqk[0:NS, 0:HW], io["s_dq"][row, :], "dq_ok", "o_dq")
            for b in range(DEC_B):
                store(t, dqk[b * DEC_T:(b + 1) * DEC_T, HW:], io["s_win_k"][b, PAST - DEC_T:PAST, :], "dk_ok", "o_dk")
            store(t, qm[0:NS], io["s_q"][row, :], "q_ok", "o_q")
            for b in range(DEC_B):
                store(t, dv[b * DEC_T:(b + 1) * DEC_T], io["s_win_v"][b, PAST - DEC_T:PAST, :], "dv_ok", "o_dv")
            for n in "o_c o_kr o_dq o_q".split():
                sp.wait_ge(S[n], 16 * NT)
            for n in "o_dk o_dv".split():
                sp.wait_ge(S[n], 16 * (PT + DEC_B))
            for n in "o_k o_v".split():
                sp.wait_ge(S[n], 16 * PT)

        @block.gpsimd
        def _(pool):
            nc.gpsimd.memset(half, -0.5).then_inc(S["p_half"], 1)
            nc.gpsimd.memset(eps, EPS).then_inc(S["p_half"], 1)
            pool.wait_ge(S["p_half"], 2)

            def rows_root(t):
                pool.wait_ge(S["x_ms"], t.n + 1)
                nc.gpsimd.tensor_tensor(xms, xms, eps[:, 0:1], ALU.add).then_inc(S["x_eps"], 1)
                pool.wait_ge(S["x_eps"], t.n + 1)
                nc.gpsimd.tensor_tensor(xrs, xms, half[:, 0:1], ALU.pow).then_inc(S["x_rs"], 1)

            def main(t):
                pool.wait_ge(S["c_ms"], t.n + 1)
                nc.gpsimd.tensor_tensor(cms, cms, eps, ALU.add).then_inc(S["c_eps"], 1)
                pool.wait_ge(S["c_eps"], t.n + 1)
                nc.gpsimd.tensor_tensor(crs, cms, half, ALU.pow).then_inc(S["c_rs"], 1)
                if not ends(t):
                    rows_root(t.after_next())

            def lead():
                rows_root(Step.of(0))
                rows_root(Step.of(1))

            staged(pool, lambda t: None, main, lead=lead)

        @block.scalar
        def _(act):
            def weights(a, b):
                for n in range(a, b):
                    act.wait_ge(S[f"wload{n % SLOTS}"], 16 * (n // SLOTS + 1))
                    nc.scalar.copy(flat(loads[n][1], n), slot(n)).then_inc(S["w_hi"], 1)

            def square(t):
                act.wait_ge(S[f"xload{t.odd}"], t.half * 16 + 16)
                if not t.first:
                    act.wait_ge(S["xT_ps"], t.n * 2)
                    act.wait_ge(S["x_rs"], t.n)
                nc.scalar.activation(xn[:], x[t.odd][:], ACT.Square, scale=D_MODEL ** -0.5,
                                     accum_out=xms).then_inc(S["x_ms"], 1)

            def prep(t):
                for i in range(2):
                    act.wait_ge(S["xT_ps"], t.n * 2 + (i + 1))
                    if not t.first and not t.second:
                        act.wait_ge(S["z3_ps"], t.n - 1)
                    nc.scalar.copy(xT_h[t.odd][:, 4 * i:4 * i + 4, :], xp[i][:]).then_inc(S["xT_hi"], 1)

            def main(t):
                act.wait_ge(S["z0_ps"], t.n + 1)
                if not t.first:
                    act.wait_ge(S["o_c"], t.n * 16)
                    act.wait_ge(S["c_rs"], t.n)
                    act.wait_ge(S["cT_ps"], t.n)
                nc.scalar.activation(cn[:, 0:Q_RANK], zp[0][:, 0:Q_RANK], ACT.Square, scale=Q_RANK ** -0.5,
                                     accum_out=cms[:, 0:1]).then_inc(S["sink"], 1)
                nc.scalar.activation(cn[:, Q_RANK:], zp[0][:, Q_RANK:Q_RANK + KV_RANK], ACT.Square,
                                     scale=KV_RANK ** -0.5, accum_out=cms[:, 1:2]).then_inc(S["c_ms"], 1)
                act.wait_ge(S["cT_ps"], t.n + 1)
                if not t.first:
                    act.wait_ge(S["kv_ps"], t.n)
                nc.scalar.copy(cT_h[:], cp[:, 0:3 * P].rearrange("p (a b) -> p a b", a=3)).then_inc(S["cT_hi"], 1)
                if not ends(t):
                    square(t.after_next())
                act.wait_ge(S["kr_ok"], t.n + 1)
                if not t.first:
                    act.wait_ge(S["o_k"], t.n * 16)
                nc.scalar.copy(km.rearrange("p (h c) -> p h c", h=HEADS)[:, :, NOPE:],
                               kr[:].unsqueeze(1).broadcast_to([P, HEADS, ROPE])).then_inc(S["k_rope"], 1)
                act.wait_ge(S["q_ps"], t.n + 1)
                if not t.first:
                    act.wait_ge(S["o_q"], t.n * 16)
                nc.scalar.copy(qm.rearrange("p (h c) -> p h c", h=HEADS)[:, :, 0:NOPE],
                               cp[:, 0:HEADS * QK].rearrange("p (h c) -> p h c", h=HEADS)[:, :, 0:NOPE])\
                    .then_inc(S["q_nope"], 1)
                act.wait_ge(S["z3_ps"], t.n + 1)
                if not t.first:
                    act.wait_ge(S["o_dv"], t.n * 16)
                nc.scalar.copy(dv, zp[3][:]).then_inc(S["dv_ok"], 1)
                act.wait_ge(S["kv_ps"], t.n + 1)
                if not t.first:
                    act.wait_ge(S["o_k"], t.n * 16)
                    act.wait_ge(S["o_v"], t.n * 16)
                nc.scalar.copy(km.rearrange("p (h c) -> p h c", h=HEADS)[:, :, 0:NOPE],
                               cp[:, 0:HW].rearrange("p (h c) -> p h c", h=HEADS)).then_inc(S["k_nope"], 1)
                nc.scalar.copy(vm[:], cp[:, 512:512 + HW]).then_inc(S["v_ok"], 1)

            def lead():
                square(Step.of(0))
                weights(0, 4)
                prep(Step.of(0))
                weights(4, 8)
                square(Step.of(1))
                prep(Step.of(1))
                weights(8, len(loads))

            staged(act, prep, main, lead=lead)

        @block.vector
        def _(dve):
            def weights(a, b):
                for n in range(a, b):
                    dve.wait_ge(S["w_hi"], n + 1)
                    nc.vector.tensor_tensor(flat(loads[n][2], n), slot(n), flat(loads[n][1], n).bitcast(F32),
                                            ALU.subtract).then_inc(S["w_lo"], 1)

            def normalize(t):
                if t.first:
                    dve.wait_ge(S["p_const"], 64)
                dve.wait_ge(S["x_rs"], t.n + 1)
                nc.vector.scalar_tensor_tensor(out=xn[:], in0=x[t.odd][:], scalar=xrs, in1=g_x[:],
                                               op0=ALU.mult, op1=ALU.mult).then_inc(S["xn_ok"], 1)

            def prep(t):
                for i in range(2):
                    dve.wait_ge(S["xT_hi"], t.n * 2 + (i + 1))
                    nc.vector.tensor_tensor(xT_l[t.odd][:, 4 * i:4 * i + 4, :], xp[i][:],
                                            xT_h[t.odd][:, 4 * i:4 * i + 4, :].bitcast(F32),
                                            ALU.subtract).then_inc(S["xT_lo"], 1)

            def rotate(src, out, tmp_a, tmp_b, table, half_n, a_sem, a_n, ok_sem):
                c = table[:, 0:2 * half_n].unsqueeze(1).broadcast_to([P, src.shape[1], 2 * half_n])
                s = table[:, 2 * half_n:3 * half_n].unsqueeze(1).broadcast_to([P, src.shape[1], half_n])
                nc.vector.tensor_tensor(tmp_a, src, c, ALU.mult).then_inc(S[a_sem], 1)
                nc.vector.tensor_tensor(tmp_b[:, :, 0:half_n], src[:, :, half_n:], s, ALU.mult).then_inc(S[a_sem], 1)
                nc.vector.tensor_tensor(tmp_b[:, :, half_n:], src[:, :, 0:half_n], s, ALU.mult).then_inc(S[a_sem], 1)
                dve.wait_ge(S[a_sem], a_n)
                nc.vector.tensor_tensor(out[:, :, 0:half_n], tmp_a[:, :, 0:half_n], tmp_b[:, :, 0:half_n],
                                        ALU.subtract).then_inc(S["sink"], 1)
                nc.vector.tensor_tensor(out[:, :, half_n:], tmp_a[:, :, half_n:], tmp_b[:, :, half_n:],
                                        ALU.add).then_inc(S[ok_sem], 1)

            def main(t):
                heads = lambda ap: ap.rearrange("p (h c) -> p h c", h=HEADS)
                dve.wait_ge(S["c_rs"], t.n + 1)
                nc.vector.scalar_tensor_tensor(out=cn[:, 0:Q_RANK], in0=zp[0][:, 0:Q_RANK], scalar=crs[:, 0:1],
                                               in1=g_c[:, 0:Q_RANK], op0=ALU.mult, op1=ALU.mult).then_inc(S["sink"], 1)
                nc.vector.scalar_tensor_tensor(out=cn[:, Q_RANK:], in0=zp[0][:, Q_RANK:Q_RANK + KV_RANK],
                                               scalar=crs[:, 1:2], in1=g_c[:, Q_RANK:], op0=ALU.mult,
                                               op1=ALU.mult).then_inc(S["cn_ok"], 1)
                if not t.first:
                    dve.wait_ge(S["o_kr"], t.n * 16)
                    dve.wait_ge(S["k_rope"], t.n)
                one = lambda ap: ap.unsqueeze(1)
                dve.wait_ge(S[f"rload{t.odd}"], t.half * 16 + 16)
                rotate(one(zp[0][:, Q_RANK + KV_RANK:G0]), one(kr[:]), one(krt[:, 0, :]), one(krt[:, 1, :]),
                       rot[t.odd][:, 3 * RD:], RM, "kr_a", t.n * 3 + 3, "kr_ok")
                for i, ok in enumerate(("dq_ok", "dk_ok")):
                    dve.wait_ge(S[f"z{i + 1}_ps"], t.n + 1)
                    if not t.first:
                        dve.wait_ge(S[("o_dq", "o_dk")[i]], t.n * 16)
                    if i == 1:
                        dve.wait_ge(S["dq_ok"], t.n + 1)
                    elif not t.first:
                        dve.wait_ge(S["dk_ok"], t.n)
                    rotate(heads(zp[i + 1][:]), heads(dqk[:, i * HW:(i + 1) * HW]), heads(rt[0]), heads(rt[1]),
                           rot[t.odd][:, 0:3 * RD], RD, "d_a", t.n * 6 + (3 * i + 3), ok)
                    if i == 0:
                        dve.wait_ge(S["cT_hi"], t.n + 1)
                        nc.vector.tensor_tensor(cT_l[:], cp[:, 0:3 * P].rearrange("p (a b) -> p a b", a=3),
                                                cT_h[:].bitcast(F32), ALU.subtract).then_inc(S["cT_lo"], 1)
                if not ends(t):
                    normalize(t.after_next())
                dve.wait_ge(S["q_nope"], t.n + 1)
                rotate(heads(cp[:, 0:HEADS * QK])[:, :, NOPE:], heads(qm)[:, :, NOPE:], qt[:, 0], qt[:, 1],
                       rot[t.odd][:, 3 * RD:], RM, "q_a", t.n * 3 + 3, "q_ok")

            def lead():
                normalize(Step.of(0))
                weights(0, 4)
                prep(Step.of(0))
                weights(4, 8)
                normalize(Step.of(1))
                prep(Step.of(1))
                weights(8, len(loads))

            staged(dve, prep, main, lead=lead)

        @block.tensor
        def _(pe):
            def prep(t):
                if t.first:
                    pe.wait_ge(S["p_const"], 64)
                pe.wait_ge(S["xn_ok"], t.n + 1)
                for i in range(2):
                    if not t.first:
                        pe.wait_ge(S["xT_lo"], t.n * 2 - (1 - i))
                    for k in range(4):
                        last = nc.tensor.transpose(xp[i][:, k, :], xn[:, (4 * i + k) * P:(4 * i + k + 1) * P], ident[:])
                    last.then_inc(S["xT_ps"], 1)

            def product(out, terms, done):
                n = len(terms) * 3
                i = 0
                for lh, ll, rh, rl in terms:
                    for a, b in ((lh, rh), (lh, rl), (ll, rh)):
                        last = nc.tensor.matmul(out, a, b, start=(i == 0), stop=(i == n - 1))
                        i += 1
                if done:
                    last.then_inc(S[done], 1)

            def group(t, g):
                c0, n = GROUPS[g]
                if t.first:
                    pe.wait_ge(S["w_lo"], need[g])
                else:
                    for s in (("kr_ok",), ("dq_ok",), ("dk_ok",), ("dv_ok",))[g]:
                        pe.wait_ge(S[s], t.n)
                product(zp[g][:, 0:n], [(xT_h[t.odd][:, k, :], xT_l[t.odd][:, k, :], win_h[:, k, c0:c0 + n],
                                         win_l[:, k, c0:c0 + n]) for k in range(KC)], f"z{g}_ps")

            def main(t):
                pe.wait_ge(S["xT_lo"], t.n * 2 + 2)
                group(t, 0)
                group(t, 1)
                pe.wait_ge(S["cn_ok"], t.n + 1)
                if not t.first:
                    pe.wait_ge(S["v_ok"], t.n)
                for i in range(3):
                    last = nc.tensor.transpose(cp[:, i * P:(i + 1) * P], cn[:, i * P:(i + 1) * P], ident[:])
                last.then_inc(S["cT_ps"], 1)
                group(t, 2)
                pe.wait_ge(S["cT_lo"], t.n + 1)
                if t.first:
                    pe.wait_ge(S["w_lo"], need["q"])
                for c0, n, done in ((0, 512, None), (512, HEADS * QK - 512, "q_ps")):
                    product(cp[:, c0:c0 + n], [(cT_h[:, k, :], cT_l[:, k, :], wqb_h[:, k, c0:c0 + n],
                                                wqb_l[:, k, c0:c0 + n]) for k in range(2)], done)
                group(t, 3)
                pe.wait_ge(S["q_ok"], t.n + 1)
                if t.first:
                    pe.wait_ge(S["w_lo"], need["kv"])
                for c0, done in ((0, None), (512, "kv_ps")):
                    product(cp[:, c0:c0 + 512], [(cT_h[:, 2, :], cT_l[:, 2, :], wkv_h[:, c0:c0 + 512],
                                                  wkv_l[:, c0:c0 + 512])], done)

            staged(pe, prep, main)


def prompt_attention(nc, sem, io):
    ctx = ExitStack()
    with ctx:
        sb = lambda n, s, d=F32: ctx.enter_context(nc.sbuf_tensor(n, s, d))
        ps = lambda n, s: ctx.enter_context(nc.psum_tensor(n, s, F32))
        qn = sb("a_qn", [P, PT, 2 * QK])
        kn = sb("a_kn", [P, PT, 2 * QK])
        vn = sb("a_vn", [P, PT, 2 * HD])
        qh, ql, kh, kl = (sb(n, [P, 2, SEQ], F32R) for n in ("a_qh", "a_ql", "a_kh", "a_kl"))
        vh, vl = (sb(n, [P, PT, 2 * HD], F32R) for n in ("a_vh", "a_vl"))
        ph, pl = (sb(n, [P, PT, 2, P], F32R) for n in ("a_ph", "a_pl"))
        pr = sb("a_pr", [P, 2, 2, SEQ])
        ot = sb("a_ot", [P, SEQ])
        table = [sb("a_causal", [P, SEQ]), sb("a_dilated", [P, SEQ])]
        ident = sb("a_ident", [P, P])
        nm = sb("a_nm", [P, 2, 2])
        den = sb("a_den", [P, 2, 2])
        rden = sb("a_rden", [P, 2, 2])
        diag = sb("a_diag", [P, 2, 2, P])
        sp_ = [ps(f"a_s{h}", [P, SEQ]) for h in range(2)]
        TB = 3
        tp = [ps(f"a_t{i}", [P, 2, 2, P]) for i in range(TB)]
        out_ps = ps("a_o", [P, 2, 2, P])
        op = [out_ps[:, i] for i in range(2)]
        S = {n: sem("a_" + n) for n in (
            "const q_in k_in v_in s_ps neg_go tr_ps tr_hi tr_lo k_lo swap v_hi v_lo neg exp recip norm t_ps t_hi t_lo "
            "o_ps o_half o_ev o_out").split()}
        GROUP = PAIRS * PT
        TR = {0: 8, 1: 4}
        units = [(j + 2) // 2 for j in range(PT)]
        before = [sum(units[:j]) for j in range(PT)]
        UNITS = sum(units)
        assert UNITS % TB == 2
        done_s, done_t = [0, GROUP], [0, PAIRS * UNITS]
        done_tr = [0, PAIRS * TR[0]]

        class At:

            def __init__(self, kind, n, start):
                self.kind, self.n = kind, n
                self.start = start
                self.steps = n * PT + done_s[kind]
                self.units = n * UNITS + done_t[kind]
                self.trs = n * TR[kind] + done_tr[kind]
                self.pair = n + PAIRS * kind

        def walk(eng, prep, steps):
            prep[0](At(0, 0, True))
            prep[1](At(0, 0, True))
            first = True
            for kind in range(2):
                if first:
                    steps(At(0, 0, True), At(0, 1, False))
                    with eng.Fori(1, PAIRS - 1) as n:
                        steps(At(0, n, False), At(0, n + 1, False))
                    steps(At(0, PAIRS - 1, False), At(1, 0, False))
                    first = False
                else:
                    with eng.Fori(0, PAIRS - 1) as n:
                        steps(At(1, n, False), At(1, n + 1, False))
                    steps(At(1, PAIRS - 1, False), None)

        def shapes(kind):
            return (QK, MLA_SCALE) if kind == 0 else (HD, DIL_SCALE)

        def parts(kind, part):
            if kind == 0:
                return [(part, h, f) for h in range(2) for f in range(2)]
            return [(part, 0, f) for f in range(2)]

        block = ctx.enter_context(nc.Block())

        @block.sync
        def _(sp):
            def load(a):
                d = QK if a.kind == 0 else HD
                c = bass.ds(a.n * 2 * d, 2 * d)
                cv = bass.ds(a.n * 2 * HD, 2 * HD)
                rows = lambda ap: ap.rearrange("(j p) c -> p j c", p=P)
                q, k, v = (io["s_q"], io["s_k"], io["s_v"]) if a.kind == 0 else (io["s_dq"], io["p_win_k"], io["p_win_v"])
                if not a.start:
                    sp.wait_ge(S["tr_ps"], a.trs)
                sp.dma_start(qn[:, :, 0:2 * d], rows(q[0:SEQ])[:, :, c]).then_inc(S["q_in"], 16)
                sp.dma_start(kn[:, :, 0:2 * d], rows(k[0:SEQ])[:, :, c]).then_inc(S["k_in"], 16)
                if not a.start:
                    sp.wait_ge(S["v_lo"], a.pair)
                sp.dma_start(vn[:], rows(v[0:SEQ])[:, :, cv]).then_inc(S["v_in"], 16)

            sp.dma_start(ident[:], io["ident"]).then_inc(S["const"], 16)
            sp.dma_start(table[0][:], io["causal"]).then_inc(S["const"], 16)
            sp.dma_start(table[1][:], io["dilated"]).then_inc(S["const"], 16)
            load(At(0, 0, True))

            def steps(a, b):
                if b is not None:
                    load(b)
                sp.wait_ge(S["o_ev"], a.steps + PT)
                sp.dma_start(io["s_o"][bass.ds(a.pair, 1), :, 0:SEQ].rearrange("o p t -> p (o t)"), ot[:])\
                    .then_inc(S["o_out"], 16)

            walk(sp, [lambda a: None] * 2, steps)
            sp.wait_ge(S["o_out"], 16 * 2 * PAIRS)

        @block.gpsimd
        def _(pool):
            def turn(b, done):
                pool.wait_ge(S["v_hi"], b + 1)
                nc.gpsimd.tensor_tensor(vl[:], vn[:], vh[:].bitcast(F32), ALU.subtract).then_inc(S["v_lo"], 1)
                pool.wait_ge(S["s_ps"], done)
                rows = lambda ap, r: ap[bass.ds(b, 1)].rearrange("o s c -> (o s) c")[r, :]
                for src, dst in (("state_win_k", "s_win_k"), ("state_win_v", "s_win_v")):
                    pool.dma_start(rows(io[dst], slice(0, PAST - DEC_T)), rows(io[src], slice(DEC_T, PAST)))\
                        .then_inc(io["moved"], 16)

            turn(0, 2)
            with pool.Fori(1, DEC_B) as b:
                turn(b, b * (2 * PT) + 2)

        @block.scalar
        def _(act):
            def prep(part):
                def run(a):
                    rows = shapes(a.kind)[0]
                    for i, (what, h, f) in enumerate(parts(a.kind, part)):
                        n = part * len(parts(a.kind, part)) + i
                        act.wait_ge(S["tr_ps"], a.trs + (n + 1))
                        bank = sp_[i // 2][:, (i % 2) * 512:(i % 2 + 1) * 512]
                        cols = slice(f * 512, f * 512 + 512)
                        if a.kind == 0:
                            nc.scalar.copy((qh, kh)[what][0:QK, h, cols], bank[0:QK]).then_inc(S["tr_hi"], 1)
                        else:
                            for e in range(2):
                                src = bank[e * HD:(e + 1) * HD]
                                if what == 1:
                                    nc.scalar.copy(kl[HD:P, e, cols], src).then_inc(S["swap"], 1)
                                last = nc.scalar.copy((qh, kh)[what][0:HD, e, cols], src)
                                last.then_inc(S["tr_hi"], 1)
                    if part == 1:
                        act.wait_ge(S["v_in"], a.pair * 16 + 16)
                        if not a.start:
                            act.wait_ge(S["o_ps"], a.steps)
                        nc.scalar.copy(vh[:], vn[:]).then_inc(S["v_hi"], 1)
                return run

            def exp(a, s):
                for h in range(2):
                    act.wait_ge(S["neg"], (a.steps + s) * 2 + (h + 1))
                    w = (s + 1) * P
                    p = pr[:, s % 2, h, 0:w]
                    nc.scalar.activation(p, p, ACT.Exp, bias=nm[:, s % 2, h:h + 1], scale=-1.0,
                                         accum_out=den[:, s % 2, h:h + 1]).then_inc(S["exp"], 1)

            def out(a, s):
                act.wait_ge(S["o_ps"], a.steps + (s + 1))
                if s == 0 and not a.start:
                    act.wait_ge(S["o_out"], a.pair * 16)
                nc.scalar.copy(ot[0:HD, s * P:(s + 1) * P], op[s % 2][0:HD, 0, :]).then_inc(S["o_half"], 1)
                nc.scalar.copy(ot[HD:P, s * P:(s + 1) * P], op[s % 2][HD:P, 1, :]).then_inc(S["o_ev"], 1)

            def high(a, s):
                for u in range(units[s]):
                    k = min(2, s + 1 - 2 * u)
                    act.wait_ge(S["t_ps"], a.units + (before[s] + u + 1))
                    if s == 0 and u == 0 and not a.start:
                        act.wait_ge(S["o_ps"], a.steps)
                    elif u == 0 and s:
                        act.wait_ge(S["o_ps"], a.steps + s)
                    nc.scalar.copy(ph[:, 2 * u:2 * u + k], tp[(before[s] + u) % TB][:, 0:k]).then_inc(S["t_hi"], 1)

            def steps(a, b):
                exp(a, 0)
                exp(a, 1)
                for s in range(PT):
                    if s:
                        out(a, s - 1)
                    high(a, s)
                    if s + 2 < PT:
                        exp(a, s + 2)
                    if s >= PT - 2 and b is not None:
                        prep(s - (PT - 2))(b)
                out(a, PT - 1)

            walk(act, [prep(0), prep(1)], steps)

        @block.vector
        def _(dve):
            dve.wait_ge(S["const"], 48)
            def prep(part):
                def run(a):
                    for i, (what, h, f) in enumerate(parts(a.kind, part)):
                        n = part * len(parts(a.kind, part)) + i
                        bank = sp_[i // 2][:, (i % 2) * 512:(i % 2 + 1) * 512]
                        cols = slice(f * 512, f * 512 + 512)
                        hi, lo = (qh, kh)[what], (ql, kl)[what]
                        if a.kind == 0:
                            dve.wait_ge(S["tr_hi"], a.trs + (n + 1))
                            nc.vector.tensor_tensor(lo[0:QK, h, cols], bank[0:QK], hi[0:QK, h, cols].bitcast(F32),
                                                    ALU.subtract).then_inc(S["tr_lo"], 1)
                            continue
                        for e in range(2):
                            dve.wait_ge(S["tr_hi"], (a.n * TR[1] + n) * 2 + (PAIRS * TR[0] + e + 1))
                            nc.vector.tensor_tensor(hi[HD:P, e, cols], bank[e * HD:(e + 1) * HD],
                                                    hi[0:HD, e, cols].bitcast(F32), ALU.subtract)\
                                .then_inc(S[("tr_lo", "k_lo")[what]], 1)
                            if what == 1:
                                dve.wait_ge(S["k_lo"], a.n * 4 + (2 * i + e + 1))
                                nc.vector.tensor_copy(lo[0:HD, e, cols], hi[HD:P, e, cols]).then_inc(S["tr_lo"], 1)
                return run

            def neg(a, s):
                w = (s + 1) * P
                for h in range(2):
                    dve.wait_ge(S["s_ps"], (a.steps + s) * 2 + (h + 1))
                    if s >= 2:
                        dve.wait_ge(S["t_ps"], a.units + before[s - 1])
                    elif not a.start:
                        dve.wait_ge(S["t_ps"], a.units)
                    dve.sem_inc(S["neg_go"])
                    nc.vector.tensor_tensor_reduce(
                        out=pr[:, s % 2, h, 0:w], in0=sp_[h][:, 0:w], in1=table[a.kind][:, SEQ - w:SEQ],
                        scale=-shapes(a.kind)[1], scalar=HUGE, op0=ALU.add, op1=ALU.min,
                        accum_out=nm[:, s % 2, h:h + 1]).then_inc(S["neg"], 1)

            def norm(a, s):
                if s >= 2:
                    dve.wait_ge(S["t_ps"], a.units + before[s - 1])
                elif not a.start:
                    dve.wait_ge(S["t_ps"], a.units)
                dve.wait_ge(S["exp"], (a.steps + s) * 2 + 2)
                nc.vector.reciprocal(rden[:, s % 2, :], den[:, s % 2, :]).then_inc(S["recip"], 1)
                dve.wait_ge(S["recip"], a.steps + (s + 1))
                for h in range(2):
                    nc.vector.tensor_scalar(diag[:, s % 2, h, :], ident[:], rden[:, s % 2, h:h + 1], None, ALU.mult)\
                        .then_inc(S["norm"], 1)

            def low(a, s):
                for u in range(units[s]):
                    k = min(2, s + 1 - 2 * u)
                    dve.wait_ge(S["t_hi"], a.units + (before[s] + u + 1))
                    nc.vector.tensor_tensor(pl[:, 2 * u:2 * u + k], tp[(before[s] + u) % TB][:, 0:k],
                                            ph[:, 2 * u:2 * u + k].bitcast(F32), ALU.subtract).then_inc(S["t_lo"], 1)

            def steps(a, b):
                if a.start:
                    dve.wait_ge(S["const"], 48)
                neg(a, 0)
                neg(a, 1)
                norm(a, 0)
                for s in range(PT):
                    low(a, s)
                    if s + 1 < PT:
                        norm(a, s + 1)
                    if s + 2 < PT:
                        neg(a, s + 2)
                    if s >= PT - 2 and b is not None:
                        prep(s - (PT - 2))(b)

            walk(dve, [prep(0), prep(1)], steps)

        @block.tensor
        def _(pe):
            def prep(part):
                def run(a):
                    if a.start and part == 0:
                        pe.wait_ge(S["const"], 48)
                    pe.wait_ge(S[("q_in", "k_in")[part]], a.pair * 16 + 16)
                    for i, (what, h, f) in enumerate(parts(a.kind, part)):
                        src = (qn, kn)[what]
                        if not (a.start and part == 0):
                            if part == 0:
                                pe.wait_ge(S["neg"], a.steps * 2)
                            else:
                                pe.wait_ge(S["tr_lo"], a.pair * 8 + 4)
                        bank = sp_[i // 2][:, (i % 2) * 512:(i % 2 + 1) * 512]
                        for j in range(4):
                            if a.kind == 0:
                                last = nc.tensor.transpose(bank[0:QK, j * P:(j + 1) * P],
                                                           src[:, 4 * f + j, h * QK:(h + 1) * QK], ident[:])
                            else:
                                last = nc.tensor.transpose(bank[:, j * P:(j + 1) * P],
                                                           src[:, 4 * f + j, 0:2 * HD], ident[:])
                        last.then_inc(S["tr_ps"], 1)
                return run

            def scores(a, s):
                rows = slice(s * P, (s + 1) * P)
                if s == 0:
                    pe.wait_ge(S["tr_lo"], a.pair * 8 + 8)
                else:
                    pe.wait_ge(S["neg"], (a.steps + s) * 2)
                for h in range(2):
                    for c in range((s + 4) // 4):
                        w = min(512, (s + 1) * P - 512 * c)
                        cols = slice(512 * c, 512 * c + w)
                        out = sp_[h][:, cols]
                        if a.kind == 0:
                            r = slice(0, QK)
                            terms = ((qh, kh), (qh, kl), (ql, kh))
                        else:
                            r = slice(0, P)
                            terms = ((qh, kh), (qh, kl))
                        for i, (x, y) in enumerate(terms):
                            last = nc.tensor.matmul(out, x[r, h, rows], y[r, h, cols], start=(i == 0),
                                                    stop=(i == len(terms) - 1))
                    last.then_inc(S["s_ps"], 1)

            def turn(a, s):
                pe.wait_ge(S["norm"], (a.steps + s) * 2 + 2)
                for u in range(units[s]):
                    k = min(2, s + 1 - 2 * u)
                    g = before[s] + u
                    if g >= TB or not a.start:
                        pe.wait_ge(S["t_lo"], a.units + (g - (TB - 1) if g >= TB else (-1, 0, 0)[g]))
                    for i in range(k):
                        for h in range(2):
                            last = nc.tensor.matmul(tp[(before[s] + u) % TB][:, i, h, :],
                                                    pr[:, s % 2, h, (2 * u + i) * P:(2 * u + i + 1) * P],
                                                    diag[:, s % 2, h, :], start=True, stop=True)
                    last.then_inc(S["t_ps"], 1)

            def value(a, s):
                if s == 0:
                    pe.wait_ge(S["v_lo"], a.pair + 1)
                if s or not a.start:
                    pe.wait_ge(S["o_ev"], a.steps + s)
                for u in range(units[s]):
                    pe.wait_ge(S["t_lo"], a.units + (before[s] + u + 1))
                    for kb in range(2 * u, min(2 * u + 2, s + 1)):
                        for i, (x, y) in enumerate(((vh, ph), (vh, pl), (vl, ph))):
                            last = nc.tensor.matmul(op[s % 2][:], x[:, kb, :], y[:, kb], start=(kb == 0 and i == 0),
                                                    stop=(kb == s and i == 2))
                last.then_inc(S["o_ps"], 1)

            def steps(a, b):
                scores(a, 0)
                scores(a, 1)
                for s in range(PT):
                    turn(a, s)
                    if s + 2 < PT:
                        scores(a, s + 2)
                    if s >= PT - 2 and b is not None:
                        prep(s - (PT - 2))(b)
                    value(a, s)

            walk(pe, [prep(0), prep(1)], steps)


def sample_latent_attention(nc, sem, io):
    H = PAGES // 4
    ctx = ExitStack()
    with ctx:
        sb = lambda n, s, d=F32: ctx.enter_context(nc.sbuf_tensor(n, s, d))
        ps = lambda n, s: ctx.enter_context(nc.psum_tensor(n, s, F32))
        ident = sb("m_ident", [P, P])
        pages = sb("m_pages", [1, DEC_B * PAGES], I32)
        wuk = sb("m_wuk", [P, HW])
        wuv = sb("m_wuv", [P, HW])
        wuv_h, wuv_l = sb("m_wuvh", [P, HW], F32R), sb("m_wuvl", [P, HW], F32R)
        ukT_h, ukT_l = sb("m_ukth", [P, PAIRS, P], F32R), sb("m_uktl", [P, PAIRS, P], F32R)
        q = sb("m_q", [NS, HEADS, QK])
        qn = sb("m_qn", [NS, HEADS, NOPE])
        qnT_h, qnT_l = sb("m_qnth", [P, PAIRS, NS], F32R), sb("m_qntl", [P, PAIRS, NS], F32R)
        q3 = sb("m_q3", [NS, HEADS, 3 * ROPE], F32R)
        ql_h, ql_l = sb("m_qlh", [P, DEC_B, NS], F32R), sb("m_qll", [P, DEC_B, NS], F32R)
        qr = sb("m_qr", [3 * ROPE, DEC_B, NS], F32R)
        qb_h, qb_l, qrb = sb("m_qbh", [P, P], F32R), sb("m_qbl", [P, P], F32R), sb("m_qrb", [3 * ROPE, P], F32R)
        cn = sb("m_cn", [DEC_T, DEC_B, P])
        cn_h, cn_l = sb("m_cnh", [DEC_T, DEC_B, P], F32R), sb("m_cnl", [DEC_T, DEC_B, P], F32R)
        nb_h, nb_l = sb("m_nbh", [DEC_T, P], F32R), sb("m_nbl", [DEC_T, P], F32R)
        cw = sb("m_cw", [NS, P])
        rw = sb("m_rw", [NS, ROPE])
        rw3 = sb("m_rw3", [NS, 3 * ROPE], F32R)
        cwT_h, cwT_l = sb("m_cwth", [P, NS], F32R), sb("m_cwtl", [P, NS], F32R)
        rwT = sb("m_rwt", [3 * ROPE, NS], F32R)
        c = [sb(f"m_c{i}", [P, PAGES, P]) for i in range(2)]
        r = [sb(f"m_r{i}", [P, PAGES, ROPE]) for i in range(2)]
        c_h, c_l = ([sb(f"m_c{x}{i}", [P, PAGES, P], F32R) for i in range(2)] for x in "hl")
        r3 = sb("m_r3", [P, PAGES, 3 * ROPE], F32R)
        cT_h, cT_l = sb("m_cth", [P, PAST], F32R), sb("m_ctl", [P, PAST], F32R)
        rT = sb("m_rt", [3 * ROPE, PAST], F32R)
        pr = [sb(f"m_p{i}", [NS, PAST + DEC_T]) for i in range(2)]
        pT_h, pT_l = sb("m_pth", [P, PAGES, NS], F32R), sb("m_ptl", [P, PAGES, NS], F32R)
        pw_h, pw_l = sb("m_pwh", [DEC_T, NS], F32R), sb("m_pwl", [DEC_T, NS], F32R)
        ol_h, ol_l = sb("m_olh", [P, HEADS, NS], F32R), sb("m_oll", [P, HEADS, NS], F32R)
        oT = sb("m_ot", [P, PAIRS, NS])
        zero = sb("m_zero", [NS, 512])
        fresh = sb("m_fresh", [NS, DEC_T])
        st = sb("m_st", [NS, 2, 8])
        tcp = [ps(f"m_tc{i}", [P, 4, P]) for i in range(2)]
        trp = ps("m_tr", [P, 4, P])
        scp = [ps(f"m_s{i}", [P, 512]) for i in range(2)]
        ptp = ps("m_pt", [P, PAGES, NS])
        op = ps("m_o", [P, 512])
        S = {n: sem("m_" + n) for n in (
            "const pages q_in new_in c_in0 c_in1 r_in0 r_in1 zeros pads qn_ok q3_h q3_l w_h w_l n_h n_l rw3_h rw3_l "
            "nb pre_ps pre_h pre_l pre2_ps pre2_h pre2_l qb r3_h r3_l c_h c_l tc_ps tc_h tc_l tr_ps tr_ev "
            "load_go load_go_r s_ps neg_go neg min exp recip norm turn_go pt_ps pt_h pt_l o_ps o_h o_l fin_ps fin_ev stored").split()}
        block = ctx.enter_context(nc.Block())
        CH = H + 1
        latent = [a.rearrange("p (i b t) -> p b i t", i=PAIRS, b=DEC_B)
                  for a in (op[:, 0:PAIRS * NS], ptp[:, 0:PAIRS].rearrange("p i n -> p (i n)"))]

        def fetch(eng, t, to, cache, done):
            for j in range(PAGES):
                page = eng.value_load(pages[0:1, bass.ds(t.n * PAGES + j, 1)], min_val=0,
                                      max_val=io[cache].shape[0] - 1)
                eng.dma_start(to[t.odd][:, j, :], io[cache][bass.ds(page, 1)].rearrange("o p c -> p (o c)"))\
                    .then_inc(S[f"{done}{t.odd}"], 16)

        mine = lambda ap, e: ap[:].rearrange("p b (i e t) -> p e b i t", i=PAIRS, e=2)[:, e]

        @block.sync
        def _(sp):
            sp.dma_start(pages[:], io["page_table"].unsqueeze(0)).then_inc(S["pages"], 16)
            sp.dma_start(ident[:], io["ident"]).then_inc(S["const"], 16)
            sp.dma_start(fresh[:], io["fresh"]).then_inc(S["const"], 16)
            sp.dma_start(wuk[:], io["w_uk"]).then_inc(S["q_in"], 16)
            sp.dma_start(q[:], io["s_q"][SEQ:TOK, :].rearrange("t (h c) -> t h c", h=HEADS)).then_inc(S["q_in"], 16)
            sp.dma_start(cw[:], io["s_kv_latent"]).then_inc(S["new_in"], 16)
            sp.dma_start(rw[:], io["s_k_rope"]).then_inc(S["new_in"], 16)
            sp.dma_start(cn[:], io["s_kv_latent"].rearrange("(b t) c -> t b c", b=DEC_B)).then_inc(S["new_in"], 16)
            sp.dma_start(wuv[:], io["w_uv"]).then_inc(S["new_in"], 16)
            sp.wait_ge(S["pages"], 16)

            def load(t):
                if not t.first and not t.second:
                    sp.wait_ge(S["c_l"], t.n - 1)
                    sp.sem_inc(S["load_go"])
                fetch(sp, t, c, "cache_kv_latent", "c_in")

            staged(sp, load, lambda t: None, DEC_B)
            sp.wait_ge(S["fin_ev"], 2)
            sp.dma_start(io["s_o"].rearrange("k p t -> p k t")[:, 0:PAIRS, SEQ:TOK], oT[:]).then_inc(S["stored"], 16)
            sp.wait_ge(S["stored"], 16)

        @block.gpsimd
        def _(pool):
            pool.wait_ge(S["pages"], 16)

            def load(t):
                if not t.first and not t.second:
                    pool.wait_ge(S["r3_l"], t.n - 1)
                    pool.sem_inc(S["load_go_r"])
                fetch(pool, t, r, "cache_k_rope", "r_in")

            staged(pool, load, lambda t: None, DEC_B)

        @block.scalar
        def _(act):
            act.wait_ge(S["q_in"], 32)
            nc.scalar.copy(qn[:], q[:, :, 0:NOPE]).then_inc(S["qn_ok"], 1)
            nc.scalar.copy(q3[:, :, 0:ROPE], q[:, :, NOPE:]).then_inc(S["q3_h"], 1)
            nc.scalar.copy(q3[:, :, ROPE:2 * ROPE], q[:, :, NOPE:]).then_inc(S["q3_h"], 1)
            act.wait_ge(S["new_in"], 64)
            nc.scalar.copy(wuv_h[:], wuv[:]).then_inc(S["w_h"], 1)
            nc.scalar.copy(cn_h[:], cn[:]).then_inc(S["n_h"], 1)
            nc.scalar.copy(rw3[:, 0:ROPE], rw[:]).then_inc(S["rw3_h"], 1)
            nc.scalar.copy(rw3[:, 2 * ROPE:], rw[:]).then_inc(S["rw3_h"], 1)
            act.wait_ge(S["pre_ps"], 2)
            nc.scalar.copy(ukT_h[:], tcp[0][:]).then_inc(S["pre_h"], 1)
            nc.scalar.copy(qnT_h[:], tcp[1][:, :, 0:NS]).then_inc(S["pre_h"], 1)
            act.wait_ge(S["pre_ps"], 3)
            nc.scalar.copy(qr[:].rearrange("p b (h t) -> p b h t", h=HEADS),
                           scp[0][0:3 * ROPE].rearrange("p (h b t) -> p b h t", h=HEADS, b=DEC_B)).then_inc(S["pre_h"], 1)
            act.wait_ge(S["pre_ps"], 4)
            nc.scalar.copy(cwT_h[:], scp[1][:, 0:NS]).then_inc(S["pre_h"], 1)
            nc.scalar.copy(rwT[:], scp[1][0:3 * ROPE, P:P + NS]).then_inc(S["pre_h"], 1)
            for e in range(2):
                act.wait_ge(S["pre2_ps"], e + 1)
                nc.scalar.copy(mine(ql_h, e), latent[e]).then_inc(S["pre2_h"], 1)

            def values(t):
                act.wait_ge(S[f"c_in{t.odd}"], t.half * 16 * PAGES + 16 * PAGES)
                if not t.first and not t.second:
                    act.wait_ge(S["o_ps"], t.n - 1)
                nc.scalar.copy(c_h[t.odd][:], c[t.odd][:]).then_inc(S["c_h"], 1)

            def new_rows(t):
                act.wait_ge(S["n_l"], 1)
                if not t.first:
                    act.wait_ge(S["o_ps"], t.n)
                new = lambda ap: ap[:, bass.ds(t.n, 1), :].rearrange("p a n -> p (a n)").bitcast(F32)
                nc.scalar.copy(nb_h[:], new(cn_h)).then_inc(S["nb"], 1)
                nc.scalar.copy(nb_l[:], new(cn_l)).then_inc(S["nb"], 1)

            def prep(t):
                if not t.first:
                    act.wait_ge(S["s_ps"], t.n * CH)
                else:
                    act.wait_ge(S["pre2_h"], 2)
                    act.wait_ge(S["pre2_l"], 2)
                    act.wait_ge(S["pre_h"], 5)
                    act.wait_ge(S["pads"], 3)
                one = lambda ap: ap[:, bass.ds(t.n, 1), :].rearrange("p a n -> p (a n)")
                nc.scalar.copy(qb_h[:, 0:NS], one(ql_h).bitcast(F32)).then_inc(S["qb"], 1)
                nc.scalar.copy(qb_l[:, 0:NS], one(ql_l).bitcast(F32)).then_inc(S["qb"], 1)
                nc.scalar.copy(qrb[:, 0:NS], one(qr).bitcast(F32)).then_inc(S["qb"], 1)
                act.wait_ge(S[f"r_in{t.odd}"], t.half * 16 * PAGES + 16 * PAGES)
                if not t.first:
                    act.wait_ge(S["tr_ps"], t.n * H)
                nc.scalar.copy(r3[:, :, 0:ROPE], r[t.odd][:]).then_inc(S["r3_h"], 1)
                nc.scalar.copy(r3[:, :, 2 * ROPE:], r[t.odd][:]).then_inc(S["r3_h"], 1)
                for h in range(H):
                    cols = slice(h * 512, h * 512 + 512)
                    act.wait_ge(S["tc_ps"], t.n * H + (h + 1))
                    nc.scalar.copy(cT_h[:, cols].rearrange("p (a b) -> p a b", a=4), tcp[h % 2][:]).then_inc(S["tc_h"], 1)
                    act.wait_ge(S["tr_ps"], t.n * H + (h + 1))
                    nc.scalar.copy(rT[:, cols].rearrange("p (a b) -> p a b", a=4), trp[0:3 * ROPE]).then_inc(S["tr_ev"], 1)
                    if h == 1:
                        values(t)
                if not t.first:
                    high(t.back)
                act.wait_ge(S["min"], t.n + 1)
                nc.scalar.activation(pr[t.odd][:], pr[t.odd][:], ACT.Exp, bias=st[:, t.odd, 5:6], scale=-1.0,
                                     accum_out=st[:, t.odd, 6:7]).then_inc(S["exp"], 1)

            def high(t):
                act.wait_ge(S["pt_ps"], t.n * 2 + 1)
                if not t.first:
                    act.wait_ge(S["o_ps"], t.n)
                nc.scalar.copy(pT_h[:, 0:8], ptp[:, 0:8]).then_inc(S["pt_h"], 1)
                act.wait_ge(S["pt_ps"], t.n * 2 + 2)
                nc.scalar.copy(pT_h[:, 8:], ptp[:, 8:]).then_inc(S["pt_h"], 1)
                nc.scalar.copy(pw_h[:], op[0:DEC_T, NS:2 * NS]).then_inc(S["pt_h"], 1)
                new_rows(t)

            def main(t):
                if t.last:
                    high(t)
                act.wait_ge(S["o_ps"], t.n + 1)
                b = bass.ds(t.n * DEC_T, DEC_T)
                nc.scalar.copy(ol_h[:, :, b], op[:, 0:NS].rearrange("p (h t) -> p h t", h=HEADS)).then_inc(S["o_h"], 1)

            staged(act, prep, main, DEC_B)
            act.wait_ge(S["fin_ps"], 1)
            o = scp[0][:].rearrange("p (i e n) -> p i e n", i=PAIRS, e=2)
            nc.scalar.copy(oT[0:HD], o[0:HD, :, 0]).then_inc(S["fin_ev"], 1)
            nc.scalar.copy(oT[HD:P], o[HD:P, :, 1]).then_inc(S["fin_ev"], 1)

        @block.vector
        def _(dve):
            dve.wait_ge(S["const"], 32)
            nc.vector.memset(zero[:], 0.0).then_inc(S["zeros"], 1)
            for a in (qb_h, qb_l, qrb):
                nc.vector.memset(a[:, NS:].bitcast(F32), 0.0).then_inc(S["pads"], 1)
            sub = lambda out, a, b: nc.vector.tensor_tensor(out, a, b.bitcast(F32), ALU.subtract)
            dve.wait_ge(S["q3_h"], 2)
            sub(q3[:, :, 2 * ROPE:], q[:, :, NOPE:], q3[:, :, 0:ROPE]).then_inc(S["q3_l"], 1)
            dve.wait_ge(S["w_h"], 1)
            sub(wuv_l[:], wuv[:], wuv_h[:]).then_inc(S["w_l"], 1)
            dve.wait_ge(S["n_h"], 1)
            sub(cn_l[:], cn[:], cn_h[:]).then_inc(S["n_l"], 1)
            dve.wait_ge(S["rw3_h"], 2)
            sub(rw3[:, ROPE:2 * ROPE], rw[:], rw3[:, 0:ROPE]).then_inc(S["rw3_l"], 1)
            dve.wait_ge(S["pre_h"], 2)
            sub(ukT_l[:], tcp[0][:], ukT_h[:]).then_inc(S["pre_l"], 1)
            sub(qnT_l[:], tcp[1][:, :, 0:NS], qnT_h[:]).then_inc(S["pre_l"], 1)
            dve.wait_ge(S["pre_h"], 5)
            sub(cwT_l[:], scp[1][:, 0:NS], cwT_h[:]).then_inc(S["pre_l"], 1)
            for e in range(2):
                dve.wait_ge(S["pre2_h"], e + 1)
                sub(mine(ql_l, e), latent[e], mine(ql_h, e)).then_inc(S["pre2_l"], 1)

            def prep(t):
                dve.wait_ge(S["r3_h"], t.n * 2 + 2)
                sub(r3[:, :, ROPE:2 * ROPE], r[t.odd][:], r3[:, :, 0:ROPE]).then_inc(S["r3_l"], 1)
                for h in range(CH):
                    if h < H:
                        cols = slice(h * 512, h * 512 + 512)
                        dve.wait_ge(S["tc_h"], t.n * H + (h + 1))
                        sub(cT_l[:, cols].rearrange("p (a b) -> p a b", a=4), tcp[h % 2][:],
                            cT_h[:, cols].rearrange("p (a b) -> p a b", a=4)).then_inc(S["tc_l"], 1)
                    if h == 0 and not t.first:
                        norm(t.back)
                    if h:
                        neg(t, h - 1)
                    if h == H - 1:
                        split(t)
                    if h == H - 1 and not t.first:
                        low(t.back)
                neg(t, CH - 1)
                dve.wait_ge(S["neg"], t.n * CH + CH)
                nc.vector.tensor_reduce(st[:, t.odd, 5:6], st[:, t.odd, 0:5], AX.X, ALU.min).then_inc(S["min"], 1)

            def neg(t, h):
                w = 512 if h < H else DEC_T
                dve.wait_ge(S["s_ps"], t.n * CH + (h + 1))
                if h == 0 and not t.first and not t.second:
                    dve.wait_ge(S["pt_ps"], t.n * 2 - 2)
                dve.sem_inc(S["neg_go"])
                nc.vector.tensor_tensor_reduce(
                    out=pr[t.odd][:, h * 512:h * 512 + w], in0=scp[h % 2][0:NS, 0:w],
                    in1=zero[:] if h < H else fresh[:], scale=-MLA_SCALE, scalar=HUGE, op0=ALU.add, op1=ALU.min,
                    accum_out=st[:, t.odd, h:h + 1]).then_inc(S["neg"], 1)

            def split(t):
                dve.wait_ge(S["c_h"], t.n + 1)
                sub(c_l[t.odd][:], c[t.odd][:], c_h[t.odd][:]).then_inc(S["c_l"], 1)

            def norm(t):
                dve.wait_ge(S["exp"], t.n + 1)
                nc.vector.reciprocal(st[:, t.odd, 7:8], st[:, t.odd, 6:7]).then_inc(S["recip"], 1)
                dve.wait_ge(S["recip"], t.n + 1)
                nc.vector.tensor_scalar(pr[t.odd][:], pr[t.odd][:], st[:, t.odd, 7:8], None, ALU.mult)\
                    .then_inc(S["norm"], 1)

            def low(t):
                dve.wait_ge(S["pt_h"], t.n * 3 + 1)
                sub(pT_l[:, 0:8], ptp[:, 0:8], pT_h[:, 0:8]).then_inc(S["pt_l"], 1)
                dve.wait_ge(S["pt_h"], t.n * 3 + 2)
                sub(pT_l[:, 8:], ptp[:, 8:], pT_h[:, 8:]).then_inc(S["pt_l"], 1)
                dve.wait_ge(S["pt_h"], t.n * 3 + 3)
                sub(pw_l[:], op[0:DEC_T, NS:2 * NS], pw_h[:]).then_inc(S["pt_l"], 1)

            def main(t):
                if t.last:
                    norm(t)
                    low(t)
                dve.wait_ge(S["o_h"], t.n + 1)
                b = bass.ds(t.n * DEC_T, DEC_T)
                sub(ol_l[:, :, b], op[:, 0:NS].rearrange("p (h t) -> p h t", h=HEADS), ol_h[:, :, b]).then_inc(S["o_l"], 1)

            staged(dve, prep, main, DEC_B)

        @block.tensor
        def _(pe):
            def product(out, terms, done=None):
                for i, (a, b) in enumerate(terms):
                    last = nc.tensor.matmul(out, a, b, start=(i == 0), stop=(i == len(terms) - 1))
                if done:
                    last.then_inc(S[done], 1)

            pe.wait_ge(S["const"], 32)
            pe.wait_ge(S["q_in"], 32)
            for i in range(PAIRS):
                last = nc.tensor.transpose(tcp[0][:, i, :], wuk[:, i * P:(i + 1) * P], ident[:])
            last.then_inc(S["pre_ps"], 1)
            pe.wait_ge(S["qn_ok"], 1)
            for i in range(PAIRS):
                last = nc.tensor.transpose(tcp[1][:, i, 0:NS], qn[:, 2 * i:2 * i + 2, :].rearrange("p a b -> p (a b)"), ident[0:NS, 0:NS])
            last.then_inc(S["pre_ps"], 1)
            pe.wait_ge(S["q3_l"], 1)
            for h in range(HEADS):
                last = nc.tensor.transpose(scp[0][0:3 * ROPE, h * NS:(h + 1) * NS], q3[:, h, :].bitcast(F32),
                                           ident[0:NS, 0:NS])
            last.then_inc(S["pre_ps"], 1)
            pe.wait_ge(S["new_in"], 64)
            pe.wait_ge(S["rw3_l"], 1)
            nc.tensor.transpose(scp[1][:, 0:NS], cw[:], ident[0:NS, 0:NS])
            nc.tensor.transpose(scp[1][0:3 * ROPE, P:P + NS], rw3[:].bitcast(F32), ident[0:NS, 0:NS])\
                .then_inc(S["pre_ps"], 1)
            pe.wait_ge(S["pre_l"], 2)
            for e in range(2):
                row = slice(e * HD, (e + 1) * HD)
                for i in range(PAIRS):
                    out = op[:, i * NS:(i + 1) * NS] if e == 0 else ptp[:, i, :]
                    product(out, ((ukT_h[row, i], qnT_h[row, i]), (ukT_h[row, i], qnT_l[row, i]),
                                  (ukT_l[row, i], qnT_h[row, i])), "pre2_ps" if i == PAIRS - 1 else None)

            def prep(t):
                if t.first:
                    pe.wait_ge(S["pre_l"], 3)
                    pe.wait_ge(S["pre_h"], 5)
                    pe.wait_ge(S["pre2_l"], 2)
                pe.wait_ge(S[f"c_in{t.odd}"], t.half * 16 * PAGES + 16 * PAGES)
                pe.wait_ge(S["r3_l"], t.n + 1)

                def turn(h):
                    if h >= 2 or not t.first:
                        pe.wait_ge(S["tc_l"], t.n * H + (h - 1))
                    for j in range(4):
                        last = nc.tensor.transpose(tcp[h % 2][:, j, :], c[t.odd][:, 4 * h + j, :], ident[:])
                    last.then_inc(S["tc_ps"], 1)
                    if h or not t.first:
                        pe.wait_ge(S["tr_ev"], t.n * H + h)
                    for j in range(4):
                        last = nc.tensor.transpose(trp[0:3 * ROPE, j, :], r3[:, 4 * h + j, :].bitcast(F32), ident[:])
                    last.then_inc(S["tr_ps"], 1)

                turn(0)
                for h in range(CH):
                    if h + 1 < H:
                        turn(h + 1)
                    if h == 0:
                        pe.wait_ge(S["qb"], t.n * 3 + 3)
                    if h >= 2 or not t.first:
                        pe.wait_ge(S["neg"], t.n * CH + (h - 1 if h else 0))
                    out = scp[h % 2]
                    if h < H:
                        cols = slice(h * 512, h * 512 + 512)
                        pe.wait_ge(S["tc_l"], t.n * H + (h + 1))
                        pe.wait_ge(S["tr_ev"], t.n * H + (h + 1))
                        x, xl, y = cT_h[:, cols], cT_l[:, cols], rT[:, cols]
                        out = out[:]
                    else:
                        b = bass.ds(t.n * DEC_T, DEC_T)
                        x, xl, y = cwT_h[:, b], cwT_l[:, b], rwT[:, b]
                        out = out[:, 0:DEC_T]
                    product(out, ((qb_h[:], x), (qb_h[:], xl), (qb_l[:], x), (qrb[:], y)), "s_ps")
                    if h == 1 and not t.first:
                        flip(t.back)

            def flip(t):
                pe.wait_ge(S["norm"], t.n + 1)
                if not t.first:
                    pe.wait_ge(S["pt_l"], t.n * 3)
                    pe.wait_ge(S["o_l"], t.n)
                pe.sem_inc(S["turn_go"])
                for j in range(PAGES):
                    last = nc.tensor.transpose(ptp[:, j, :], pr[t.odd][:, j * P:(j + 1) * P], ident[0:NS, 0:NS])
                    if j == 7:
                        last.then_inc(S["pt_ps"], 1)
                nc.tensor.transpose(op[0:DEC_T, NS:2 * NS], pr[t.odd][:, PAST:PAST + DEC_T], ident[0:NS, 0:NS])\
                    .then_inc(S["pt_ps"], 1)

            def main(t):
                if t.last:
                    flip(t)
                pe.wait_ge(S["c_l"], t.n + 1)
                pe.wait_ge(S["pt_l"], t.n * 3 + 3)
                pe.wait_ge(S["nb"], t.n * 2 + 2)
                terms = []
                for j in range(PAGES):
                    ch, cl = c_h[t.odd][:, j, :], c_l[t.odd][:, j, :]
                    terms += [(ch, pT_h[:, j, :]), (ch, pT_l[:, j, :]), (cl, pT_h[:, j, :])]
                terms += [(nb_h[:], pw_h[:]), (nb_h[:], pw_l[:]), (nb_l[:], pw_h[:])]
                product(op[:, 0:NS], terms, "o_ps")

            staged(pe, prep, main, DEC_B)
            pe.wait_ge(S["o_l"], DEC_B)
            pe.wait_ge(S["w_l"], 1)
            pe.wait_ge(S["neg"], DEC_B * CH)
            for h in range(HEADS):
                cols = slice(h // 2 * P, h // 2 * P + P)
                product(scp[0][:, h * NS:(h + 1) * NS], ((wuv_h[:, cols], ol_h[:, h]), (wuv_h[:, cols], ol_l[:, h]),
                                                         (wuv_l[:, cols], ol_h[:, h])),
                        "fin_ps" if h == HEADS - 1 else None)


def sample_window_attention(nc, sem, io):
    FAR = 4 * FAR_ROWS
    UNIT = (FAR, FAR + DEC_T, 512)
    AT = (0, FAR, 2 * FAR + DEC_T)
    N = 3 * PAIRS
    FLIP, HIGH = 6, 8
    STEP = P + 2 * DEC_T
    ctx = ExitStack()
    with ctx:
        sb = lambda n, s, d=F32: ctx.enter_context(nc.sbuf_tensor(n, s, d))
        ps = lambda n, s: ctx.enter_context(nc.psum_tensor(n, s, F32))
        ident = sb("w_ident", [P, P])
        window = sb("w_window", [NS, WIN_KEYS])
        own = sb("w_own", [NS, HW])
        q = sb("w_q", [NS, HW])
        qT_h, qT_l = sb("w_qth", [P, PAIRS, NS], F32R), sb("w_qtl", [P, PAIRS, NS], F32R)
        qb_h, qb_l = sb("w_qbh", [P, PAIRS * STEP], F32R), sb("w_qbl", [P, PAIRS * STEP], F32R)
        kf = [sb(f"w_kf{i}", [FAR_ROWS, DEC_T, HW]) for i in range(2)]
        kn = [sb(f"w_kn{i}", [P, NEAR, HW]) for i in range(2)]
        kw = [sb(f"w_kw{i}", [DEC_T, HW]) for i in range(2)]
        vf, vn, vw = sb("w_vf", [FAR_ROWS, DEC_T, HW]), sb("w_vn", [P, NEAR, HW]), sb("w_vw", [DEC_T, HW])
        vf_h, vn_h, vw_h = (sb(n, s, F32R) for n, s in (("w_vfh", [FAR_ROWS, DEC_T, HW]), ("w_vnh", [P, NEAR, HW]),
                                                        ("w_vwh", [DEC_T, HW])))
        vf_l, vn_l, vw_l = (sb(n, s, F32R) for n, s in (("w_vfl", [FAR_ROWS, DEC_T, HW]), ("w_vnl", [P, NEAR, HW]),
                                                        ("w_vwl", [DEC_T, HW])))
        kT_h = [sb(f"w_kth{i}", [P, 512], F32R) for i in range(2)]
        kT_l = [sb(f"w_ktl{i}", [P, 512], F32R) for i in range(2)]
        pr = [sb(f"w_p{i}", [NS, WIN_KEYS]) for i in range(2)]
        pf_h, pf_l = sb("w_pfh", [FAR_ROWS, DEC_T + 1, NS], F32R), sb("w_pfl", [FAR_ROWS, DEC_T + 1, NS], F32R)
        pn_h, pn_l = sb("w_pnh", [P, NEAR + 1, NS], F32R), sb("w_pnl", [P, NEAR + 1, NS], F32R)
        pw_h, pw_l = sb("w_pwh", [DEC_T, 2, NS], F32R), sb("w_pwl", [DEC_T, 2, NS], F32R)
        o = sb("w_o", [NS, HW])
        oT = sb("w_ot", [P, PAIRS, NS])
        st = sb("w_st", [NS, 2, 6])
        tp = [ps(f"w_t{i}", [P, 512]) for i in range(2)]
        scp = [ps(f"w_s{i}", [P, 512]) for i in range(3)]
        pfp, pnp = ps("w_pf", [P, DEC_T, NS]), ps("w_pn", [P, NEAR + 1, NS])
        op = ps("w_op", [P, 512])
        S = {n: sem("w_" + n) for n in (
            "const q_in k_in0 k_in1 v_in pads turn_go neg_go q_ps q_h q_l qb tr_ps tr_h tr_l sc_ps neg min exp recip norm v_h vf_l vn_l vw_l "
            "pf_ps pn_ps p_h p_l o_ps o_ok f_ps f_ok stored").split()}
        block = ctx.enter_context(nc.Block())

        @block.sync
        def _(sp):
            sp.dma_start(ident[:], io["ident"]).then_inc(S["const"], 16)
            sp.dma_start(window[:], io["window"]).then_inc(S["const"], 16)
            sp.dma_start(own[:], io["own"]).then_inc(S["const"], 16)
            sp.dma_start(q[:], io["s_dq"][SEQ:TOK, :]).then_inc(S["q_in"], 16)

            def rows(t, src, new, far, near, fresh, done):
                seq = lambda ap: ap[bass.ds(t.n, 1)].rearrange("o s c -> (o s) c")
                sp.dma_start(far[:], seq(io[src])[0:PAST - 512, :].rearrange("(g r) c -> g r c", r=16)[:, 0:DEC_T, :])\
                    .then_inc(S[done], 16)
                sp.dma_start(near[:], seq(io[src])[PAST - 512:PAST, :].rearrange("(p u) c -> p u c", u=NEAR))\
                    .then_inc(S[done], 16)
                sp.dma_start(fresh[:], seq(io[new])[PAST - DEC_T:PAST, :]).then_inc(S[done], 16)

            def prep(t):
                if not t.first and not t.second:
                    sp.wait_ge(S["tr_ps"], t.n * N - N)
                rows(t, "state_win_k", "s_win_k", kf[t.odd], kn[t.odd], kw[t.odd], f"k_in{t.odd}")

            def main(t):
                if not t.first:
                    sp.wait_ge(S["vf_l"], t.n * 2)
                    sp.wait_ge(S["vn_l"], t.n)
                rows(t, "state_win_v", "s_win_v", vf, vn, vw, "v_in")

            staged(sp, prep, main, DEC_B)
            sp.wait_ge(S["f_ok"], DEC_B)
            sp.dma_start(io["s_o"].rearrange("k p t -> p k t")[:, PAIRS:, SEQ:TOK], oT[:]).then_inc(S["stored"], 16)
            sp.wait_ge(S["stored"], 16)

        @block.gpsimd
        def _(pool):
            def low(t):
                for part in range(2):
                    half = slice(part * 4, part * 4 + 4)
                    pool.wait_ge(S["v_h"], t.n * 4 + (part + 1))
                    nc.gpsimd.tensor_tensor(vf_l[:, half], vf[:, half], vf_h[:, half].bitcast(F32), ALU.subtract)\
                        .then_inc(S["vf_l"], 1)

            staged(pool, low, lambda t: None, DEC_B)

        @block.scalar
        def _(act):
            act.wait_ge(S["q_ps"], 1)
            nc.scalar.copy(qT_h[:], tp[0][:, 0:PAIRS * NS].rearrange("p (i n) -> p i n", i=PAIRS)).then_inc(S["q_h"], 1)

            def values(t, part):
                if part < 2:
                    if part == 0:
                        act.wait_ge(S["v_in"], t.n * 48 + 48)
                        if not t.first:
                            act.wait_ge(S["o_ps"], t.n)
                    half = slice(part * 4, part * 4 + 4)
                    nc.scalar.copy(vf_h[:, half], vf[:, half]).then_inc(S["v_h"], 1)
                else:
                    nc.scalar.copy(vn_h[:], vn[:]).then_inc(S["v_h"], 1)
                    nc.scalar.copy(vw_h[:], vw[:]).then_inc(S["v_h"], 1)

            def prep(t):
                if t.first:
                    act.wait_ge(S["q_l"], 1)
                    act.wait_ge(S["q_h"], 1)
                    act.wait_ge(S["pads"], 8)
                else:
                    act.wait_ge(S["sc_ps"], t.n * N)
                for qb, qT in ((qb_h, qT_h), (qb_l, qT_l)):
                    for e in range(2):
                        rows = slice(e * HD, (e + 1) * HD)
                        nc.scalar.copy(qb[rows].rearrange("p (i n) -> p i n", i=PAIRS)[:, :, e * DEC_T:(e + 1) * DEC_T],
                                       qT[rows, :, bass.ds(t.n * DEC_T, DEC_T)].bitcast(F32)).then_inc(S["qb"], 1)
                for n in range(N):
                    if n in (2, 4, 6) and not t.first:
                        values(t.back, n // 2 - 1)
                    w = UNIT[n % 3]
                    act.wait_ge(S["tr_ps"], t.n * N + (n + 1))
                    if n >= 2 or not t.first:
                        act.wait_ge(S["sc_ps"], t.n * N + (n - 1))
                    nc.scalar.copy(kT_h[n % 2][:, 0:w], tp[n % 2][:, 0:w]).then_inc(S["tr_h"], 1)
                    if n == HIGH and not t.first:
                        high(t.back)
                act.wait_ge(S["min"], t.n + 1)
                nc.scalar.activation(pr[t.odd][:], pr[t.odd][:], ACT.Exp, bias=st[:, t.odd, 3:4], scale=-1.0,
                                     accum_out=st[:, t.odd, 4:5]).then_inc(S["exp"], 1)

            def main(t):
                if t.last:
                    for part in range(3):
                        values(t, part)
                    high(t)

            def high(t):
                if not t.first:
                    act.wait_ge(S["o_ps"], t.n)
                act.wait_ge(S["pf_ps"], t.n + 1)
                nc.scalar.copy(pf_h[:, 0:DEC_T], pfp[0:FAR_ROWS]).then_inc(S["p_h"], 1)
                act.wait_ge(S["pn_ps"], t.n + 1)
                nc.scalar.copy(pn_h[:, 0:NEAR], pnp[:, 0:NEAR]).then_inc(S["p_h"], 1)
                nc.scalar.copy(pw_h[:, 0], pnp[0:DEC_T, NEAR]).then_inc(S["p_h"], 1)

            staged(act, prep, main, DEC_B)

        @block.vector
        def _(dve):
            dve.wait_ge(S["const"], 48)
            for a in (qb_h, qb_l):
                nc.vector.memset(a[:].bitcast(F32), 0.0).then_inc(S["pads"], 1)
            for a, n in ((pf_h, DEC_T), (pf_l, DEC_T), (pn_h, NEAR), (pn_l, NEAR), (pw_h, 1), (pw_l, 1)):
                nc.vector.memset(a[:, n:n + 1].bitcast(F32), 0.0).then_inc(S["pads"], 1)
            sub = lambda out, a, b: nc.vector.tensor_tensor(out, a, b.bitcast(F32), ALU.subtract)
            dve.wait_ge(S["q_h"], 1)
            sub(qT_l[:], tp[0][:, 0:PAIRS * NS].rearrange("p (i n) -> p i n", i=PAIRS), qT_h[:]).then_inc(S["q_l"], 1)

            def values(t):
                dve.wait_ge(S["v_h"], t.n * 4 + 4)
                sub(vn_l[:], vn[:], vn_h[:]).then_inc(S["vw_l"], 1)
                sub(vw_l[:], vw[:], vw_h[:]).then_inc(S["vn_l"], 1)

            def prep(t):
                for n in range(N):
                    w = UNIT[n % 3]
                    dve.wait_ge(S["tr_h"], t.n * N + (n + 1))
                    sub(kT_l[n % 2][:, 0:w], tp[n % 2][:, 0:w], kT_h[n % 2][:, 0:w]).then_inc(S["tr_l"], 1)
                    if n == 1 and not t.first:
                        one_over(t.back)
                        if not t.second:
                            collect(t.back.n - 1)
                    if n == 7 and not t.first:
                        values(t.back)
                    if n == HIGH and not t.first:
                        low(t.back)
                for u in range(3):
                    dve.wait_ge(S["sc_ps"], t.n * N + (N - 2 + u))
                    if not t.first and not t.second:
                        dve.wait_ge(S["pn_ps"], t.n - 1)
                    dve.sem_inc(S["neg_go"])
                    cols = slice(AT[u], AT[u] + UNIT[u])
                    nc.vector.tensor_tensor_reduce(
                        out=pr[t.odd][:, cols], in0=scp[u][0:NS, 0:UNIT[u]], in1=window[:, cols], scale=-DIL_SCALE,
                        scalar=HUGE, op0=ALU.add, op1=ALU.min, accum_out=st[:, t.odd, u:u + 1]).then_inc(S["neg"], 1)
                dve.wait_ge(S["neg"], t.n * 3 + 3)
                nc.vector.tensor_reduce(st[:, t.odd, 3:4], st[:, t.odd, 0:3], AX.X, ALU.min).then_inc(S["min"], 1)

            def one_over(t):
                dve.wait_ge(S["exp"], t.n + 1)
                nc.vector.reciprocal(st[:, t.odd, 5:6], st[:, t.odd, 4:5]).then_inc(S["recip"], 1)

            def low(t):
                dve.wait_ge(S["p_h"], t.n * 3 + 1)
                sub(pf_l[:, 0:DEC_T], pfp[0:FAR_ROWS], pf_h[:, 0:DEC_T]).then_inc(S["p_l"], 1)
                dve.wait_ge(S["p_h"], t.n * 3 + 3)
                sub(pn_l[:, 0:NEAR], pnp[:, 0:NEAR], pn_h[:, 0:NEAR]).then_inc(S["p_l"], 1)
                sub(pw_l[:, 0], pnp[0:DEC_T, NEAR], pw_h[:, 0]).then_inc(S["p_l"], 1)

            def main(t):
                if t.last:
                    one_over(t)
                    collect(t.n - 1)
                    values(t)
                    low(t)
                dve.wait_ge(S["recip"], t.n + 1)
                dve.wait_ge(S["o_ps"], t.n + 1)
                if not t.first:
                    dve.wait_ge(S["f_ps"], t.n)
                nc.vector.scalar_tensor_tensor(o[:], op[0:NS], st[:, t.odd, 5:6], own[:], ALU.mult, ALU.mult)\
                    .then_inc(S["o_ok"], 1)
                if t.last:
                    collect(t.n)

            def collect(n):
                dve.wait_ge(S["f_ps"], n + 1)
                nc.vector.tensor_reduce(oT[:, :, bass.ds(n * DEC_T, DEC_T)],
                                        pfp[:, 0:PAIRS].rearrange("p i (h t) -> p i t h", h=HEADS), AX.X, ALU.add)\
                    .then_inc(S["f_ok"], 1)

            staged(dve, prep, main, DEC_B)

        @block.tensor
        def _(pe):
            pe.wait_ge(S["const"], 48)
            pe.wait_ge(S["q_in"], 16)
            for i in range(PAIRS):
                last = nc.tensor.transpose(tp[0][:, i * NS:(i + 1) * NS], q[:, i * P:(i + 1) * P], ident[0:NS, 0:NS])
            last.then_inc(S["q_ps"], 1)

            def prep(t):
                if t.first:
                    pe.wait_ge(S["q_l"], 1)
                pe.wait_ge(S[f"k_in{t.odd}"], t.half * 48 + 48)

                def turn(n):
                    i, u = n // 3, n % 3
                    cols = slice(i * P, (i + 1) * P)
                    if n >= 2 or not t.first:
                        pe.wait_ge(S["tr_l"], t.n * N + (n - 1))
                    if u < 2:
                        tiles = [(j * FAR_ROWS, kf[t.odd][:, 4 * u + j, cols], FAR_ROWS) for j in range(4)]
                        if u == 1:
                            tiles.append((FAR, kw[t.odd][:, cols], DEC_T))
                    else:
                        tiles = [(j * P, kn[t.odd][:, j, cols], P) for j in range(4)]
                    for at, src, r in tiles:
                        last = nc.tensor.transpose(tp[n % 2][:, at:at + r], src, ident[0:r, 0:r])
                    last.then_inc(S["tr_ps"], 1)

                turn(0)
                for n in range(N):
                    if n + 1 < N:
                        turn(n + 1)
                    i, u = n // 3, n % 3
                    if n == 0:
                        pe.wait_ge(S["qb"], t.n * 4 + 4)
                    if i == 0 and not t.first:
                        pe.wait_ge(S["neg"], t.n * 3 - (2 - u))
                    pe.wait_ge(S["tr_l"], t.n * N + (n + 1))
                    w = UNIT[u]
                    x = slice(i * P, (i + 1) * P)
                    for j, (a, b) in enumerate(((qb_h, kT_h), (qb_h, kT_l), (qb_l, kT_h))):
                        last = nc.tensor.matmul(scp[u][:, 0:w], a[:, x], b[n % 2][:, 0:w], start=(i == 0 and j == 0),
                                                stop=(i == PAIRS - 1 and j == 2))
                    last.then_inc(S["sc_ps"], 1)
                    if n == 0 and not t.first and not t.second:
                        finish(t.back.n - 1)
                    if n == FLIP and not t.first:
                        flip(t.back)

            def flip(t):
                pe.wait_ge(S["exp"], t.n + 1)
                if not t.first:
                    pe.wait_ge(S["f_ok"], t.n)
                pe.sem_inc(S["turn_go"])
                p = pr[t.odd]
                for r in range(DEC_T):
                    last = nc.tensor.transpose(pfp[0:FAR_ROWS, r, :], p[:, r * FAR_ROWS:(r + 1) * FAR_ROWS],
                                               ident[0:NS, 0:NS])
                last.then_inc(S["pf_ps"], 1)
                for u in range(NEAR):
                    nc.tensor.transpose(pnp[:, u, :], p[:, AT[2] + u * P:AT[2] + (u + 1) * P], ident[0:NS, 0:NS])
                nc.tensor.transpose(pnp[0:DEC_T, NEAR, :], p[:, 2 * FAR:2 * FAR + DEC_T], ident[0:NS, 0:NS])\
                    .then_inc(S["pn_ps"], 1)

            def main(t):
                if t.last:
                    finish(t.n - 1)
                    flip(t)
                if not t.first:
                    pe.wait_ge(S["o_ok"], t.n)
                flat = lambda ap: ap.rearrange("p a n -> p (a n)")
                pe.wait_ge(S["p_l"], t.n * 3 + 3)
                pe.wait_ge(S["vn_l"], t.n + 1)
                pe.wait_ge(S["vf_l"], t.n * 2 + 2)
                tiles = [((pf_h, pf_l), r, vf_h[:, r], vf_l[:, r]) for r in range(DEC_T)]
                tiles += [((pn_h, pn_l), u, vn_h[:, u], vn_l[:, u]) for u in range(NEAR)]
                tiles += [((pw_h, pw_l), 0, vw_h[:], vw_l[:])]
                for n, ((ph, pl), r, vh, vl) in enumerate(tiles):
                    for j, (a, b) in enumerate(((ph, vh), (ph, vl), (pl, vh))):
                        last = nc.tensor.matmul(op[:], flat(a[:, r:r + 2, :]), b, start=(n == 0 and j == 0),
                                                stop=(n == len(tiles) - 1 and j == 2))
                last.then_inc(S["o_ps"], 1)
                if t.last:
                    finish(t.n)

            def finish(n):
                pe.wait_ge(S["o_ok"], n + 1)
                pe.sem_inc(S["turn_go"])
                for i in range(PAIRS):
                    last = nc.tensor.transpose(pfp[:, i, :], o[:, i * P:(i + 1) * P], ident[0:NS, 0:NS])
                last.then_inc(S["f_ps"], 1)

            staged(pe, prep, main, DEC_B)


def output_projection(nc, sem, io):
    acc, hT_h, hT_l = io["acc"], io["hT_h"], io["hT_l"]
    ctx = ExitStack()
    with ctx:
        sb = lambda n, s, d=F32: ctx.enter_context(nc.sbuf_tensor(n, s, d))
        ps = lambda n, s: ctx.enter_context(nc.psum_tensor(n, s, F32))
        wh = sb("o_wh", [P, KC, D_MODEL], F32R)
        wl = sb("o_wl", [P, KC, D_MODEL], F32R)
        work = sb("o_work", [P, 2, D_MODEL])
        stage = work[:, 0, :].rearrange("p (k t) -> p k t", k=KC)
        hn = work[:, 1, :]
        oT_h = [sb(f"o_th{i}", [P, KC, P], F32R) for i in range(2)]
        oT_l = [sb(f"o_tl{i}", [P, KC, P], F32R) for i in range(2)]
        g = sb("o_g", [P, D_MODEL])
        ident = sb("o_ident", [P, P])
        st = sb("o_st", [P, 4])
        ms, rs, half, eps = (st[:, i:i + 1] for i in range(4))
        mp = [ps(f"o_m{i}", [P, D_MODEL]) for i in range(2)]
        xp = [ps(f"o_x{i}", [P, 4, P]) for i in range(2)]
        S = {n: sem("o_" + n) for n in (
            "const x_in w_in0 w_in1 w_in2 w_in3 w_in4 w_in5 w_in6 w_in7 t_in w_hi w_lo t_hi t_lo m_ps h_ok ms eps rs hn_ok x_ps x_hi x_lo c_half pad").split()}
        ends = lambda t: isinstance(t.n, int) and t.n > NT - 3
        block = ctx.enter_context(nc.Block())

        @block.sync
        def _(sp):
            w = io["w_out"].rearrange("(k p) n -> p k n", p=P)
            def load(t, cols, n):
                if not t.first:
                    sp.wait_ge(S["t_lo"], t.n)
                sp.dma_start(stage[:, :, 0:n], io["s_o"].rearrange("k p t -> p k t")[:, :, cols]).then_inc(S["t_in"], 16)

            load(Step.of(0), slice(0, P), P)
            for k in range(KC):
                sp.dma_start(acc[:, k, :], w[:, k, :]).then_inc(S[f"w_in{k}"], 16)
            sp.dma_start(ident[:], io["ident"]).then_inc(S["const"], 16)
            sp.dma_start(g[:], io["g_ffn"].partition_broadcast(P)).then_inc(S["const"], 16)
            sp.dma_start(acc[0:NS, PT, :], io["x_sample"]).then_inc(S["x_in"], 16)
            load(Step.of(1), slice(P, 2 * P), P)
            sp.wait_ge(S["w_lo"], KC)
            sp.dma_start(acc[:, 0:PT, :], io["x_prompt"].rearrange("(t p) d -> p t d", p=P)).then_inc(S["x_in"], 16)
            with sp.Fori(2, PT) as n:
                load(Step(n, None, None), bass.ds(n * P, P), P)
            load(Step.of(PT), slice(SEQ, TOK), NS)

        @block.gpsimd
        def _(pool):
            nc.gpsimd.memset(half, -0.5).then_inc(S["c_half"], 1)
            nc.gpsimd.memset(eps, EPS).then_inc(S["c_half"], 1)
            pool.wait_ge(S["c_half"], 2)

            def main(t):
                pool.wait_ge(S["ms"], t.n + 1)
                nc.gpsimd.tensor_tensor(ms, ms, eps, ALU.add).then_inc(S["eps"], 1)
                pool.wait_ge(S["eps"], t.n + 1)
                nc.gpsimd.tensor_tensor(rs, ms, half, ALU.pow).then_inc(S["rs"], 1)

            main(Step.of(0))
            with pool.Fori(1, NT) as n:
                main(Step(n, None, None))

        @block.scalar
        def _(act):

            def split(t):
                act.wait_ge(S["t_in"], t.n * 16 + 16)
                if not t.first and not t.second:
                    act.wait_ge(S["m_ps"], t.n - 1)
                nc.scalar.copy(oT_h[t.odd][:], stage).then_inc(S["t_hi"], 1)

            def main(t):
                act.wait_ge(S["h_ok"], t.n + 1)
                if not t.first:
                    act.wait_ge(S["x_ps"], t.n * 2)
                    act.wait_ge(S["rs"], t.n)
                nc.scalar.activation(hn, acc[:, bass.ds(t.n, 1), :].rearrange("p a d -> p (a d)"), ACT.Square,
                                     scale=D_MODEL ** -0.5, accum_out=ms).then_inc(S["ms"], 1)
                if not ends(t):
                    split(t.after_next())
                for i in range(2):
                    act.wait_ge(S["x_ps"], t.n * 2 + (i + 1))
                    n = P if not t.last else NS
                    nc.scalar.copy(hT_h[:, 4 * i:4 * i + 4, bass.ds(t.n * P, n)], xp[i][:, :, 0:n]).then_inc(S["x_hi"], 1)

            def lead():
                split(Step.of(0))
                for k in range(KC):
                    act.wait_ge(S[f"w_in{k}"], 16)
                    nc.scalar.copy(wh[:, k, :], acc[:, k, :]).then_inc(S["w_hi"], 1)
                split(Step.of(1))

            staged(act, lambda t: None, main, lead=lead)

        @block.vector
        def _(dve):
            nc.vector.memset(acc[NS:P, PT, :], 0.0).then_inc(S["pad"], 1)

            def split(t):
                dve.wait_ge(S["t_hi"], t.n + 1)
                nc.vector.tensor_tensor(oT_l[t.odd][:], stage, oT_h[t.odd][:].bitcast(F32),
                                        ALU.subtract).then_inc(S["t_lo"], 1)

            def main(t):
                if t.first:
                    dve.wait_ge(S["x_in"], 32)
                    dve.wait_ge(S["const"], 32)
                    dve.wait_ge(S["pad"], 1)
                dve.wait_ge(S["m_ps"], t.n + 1)
                h = acc[:, bass.ds(t.n, 1), :].rearrange("p a d -> p (a d)")
                nc.vector.tensor_tensor(h, mp[t.odd][:], h, ALU.add).then_inc(S["h_ok"], 1)
                dve.wait_ge(S["rs"], t.n + 1)
                nc.vector.scalar_tensor_tensor(out=hn, in0=h, scalar=rs, in1=g[:], op0=ALU.mult,
                                               op1=ALU.mult).then_inc(S["hn_ok"], 1)
                if not ends(t):
                    split(t.after_next())
                for i in range(2):
                    dve.wait_ge(S["x_hi"], t.n * 2 + (i + 1))
                    n = P if not t.last else NS
                    cols = bass.ds(t.n * P, n)
                    nc.vector.tensor_tensor(hT_l[:, 4 * i:4 * i + 4, cols], xp[i][:, :, 0:n],
                                            hT_h[:, 4 * i:4 * i + 4, cols].bitcast(F32),
                                            ALU.subtract).then_inc(S["x_lo"], 1)

            def lead():
                split(Step.of(0))
                for k in range(KC):
                    dve.wait_ge(S["w_hi"], k + 1)
                    nc.vector.tensor_tensor(wl[:, k, :], acc[:, k, :], wh[:, k, :].bitcast(F32),
                                            ALU.subtract).then_inc(S["w_lo"], 1)
                split(Step.of(1))

            staged(dve, lambda t: None, main, lead=lead)

        @block.tensor
        def _(pe):
            def prep(t):
                pe.wait_ge(S["t_lo"], t.n + 1)
                if not t.first and not t.second:
                    pe.wait_ge(S["h_ok"], t.n - 1)
                for c in range(2):
                    cols = slice(c * 512, c * 512 + 512)
                    for k in range(KC):
                        if t.first and c == 0:
                            pe.wait_ge(S["w_lo"], k + 1)
                        for i, (a, b) in enumerate(((oT_h, wh), (oT_h, wl), (oT_l, wh))):
                            last = nc.tensor.matmul(mp[t.odd][:, cols], a[t.odd][:, k, :], b[:, k, cols],
                                                    start=(k == 0 and i == 0), stop=(k == KC - 1 and i == 2))
                last.then_inc(S["m_ps"], 1)

            def main(t):
                pe.wait_ge(S["hn_ok"], t.n + 1)
                for i in range(2):
                    if not t.first:
                        pe.wait_ge(S["x_lo"], t.n * 2 - (1 - i))
                    for k in range(4):
                        last = nc.tensor.transpose(xp[i][:, k, :], hn[:, (4 * i + k) * P:(4 * i + k + 1) * P], ident[:])
                    last.then_inc(S["x_ps"], 1)

            staged(pe, prep, main)


def gated_mlp(nc, sem, io):
    acc, hT_h, hT_l = io["acc"], io["hT_h"], io["hT_l"]
    PAD = NT * P
    COEF = DEC_B * (CONV_W - 1) + CONV_W + 1
    LASTS = (DEC_B + 1) * (CONV_W - 1)
    ITER = FC // 2
    MAIN = 832
    REST, SAMPLE = TOK - MAIN, SEQ - MAIN
    ctx = ExitStack()
    with ctx:
        sb = lambda n, s, d=F32: ctx.enter_context(nc.sbuf_tensor(n, s, d))
        ps = lambda n, s: ctx.enter_context(nc.psum_tensor(n, s, F32))
        w_raw = {n: sb(f"f_{n}raw", [P, KC, P]) for n in "gu"}
        w_hi = {n: sb(f"f_{n}h", [P, KC, P], F32R) for n in "gu"}
        w_lo = {n: sb(f"f_{n}l", [P, KC, P], F32R) for n in "gu"}
        d_raw = sb("f_draw", [P, 2, D_MODEL])
        d_hi = sb("f_dh", [P, 2, D_MODEL], F32R)
        d_lo = sb("f_dl", [P, 2, D_MODEL], F32R)
        a_hi = sb("f_ah", [P, 2, PAD], F32R)
        a_lo = sb("f_al", [P, 2, PAD], F32R)
        gc = sb("f_gc", [P, TOK])
        sg = sb("f_sg", [P, TOK])
        gx = sb("f_gx", [P, DEC_B, DEC_T + CONV_W - 1])
        rows = sb("f_rows", [COEF, D_FF])
        coef = sb("f_coef", [P, FC, COEF])
        lasts = sb("f_lasts", [P, FC, LASTS])
        g = sb("f_g", [P, D_MODEL])
        ident = sb("f_ident", [P, P])
        st = sb("f_st", [P, 2 * NT + 2])
        ms, rs = ([st[:, a * NT + t:a * NT + t + 1] for t in range(NT)] for a in range(2))
        half, eps = st[:, 2 * NT:2 * NT + 1], st[:, 2 * NT + 1:2 * NT + 2]
        gp, up = ps("f_gp", [P, SEQ]), ps("f_up", [P, SEQ])
        gsp, usp = ps("f_gsp", [P, 512]), ps("f_usp", [P, 512])
        dp = [ps(f"f_dp{i}", [P, 512]) for i in range(2)]
        S = {n: sem("f_" + n) for n in (
            "const rows g_in u_in d_in g_hi u_hi d_hi g_lo u_lo d_lo g_ps u_ps d_ps coef_ps coef copied gx_ok tap1 conv "
            "conv_s1 conv_s silu mul_s mul a_hi a_lo d_add pad c_half ms eps rs y_ok out out0 out1 last_ps last_ev sink").split()}
        DT = NT * 2
        block = ctx.enter_context(nc.Block())
        taps = DEC_B * (CONV_W - 1)

        def sweep(eng, first, body, end, tail):
            first(0)
            with eng.Fori(1, ITER - 1) as i:
                body(i)
            end(ITER - 1)
            tail(ITER)

        @block.sync
        def _(sp):
            wsrc = {"g": io["w_gate"].rearrange("(k p) n -> p k n", p=P), "u": io["w_up"].rearrange("(k p) n -> p k n", p=P)}

            def load(n, f, start=False):
                if not start:
                    sp.wait_ge(S[n + "_lo"], f)
                sp.dma_start(w_raw[n][:], wsrc[n][:, :, bass.ds(f * P, P)]).then_inc(S[n + "_in"], 16)

            def load_d(i, start=False):
                if not start:
                    sp.wait_ge(S["d_lo"], i)
                sp.dma_start(d_raw[:], io["w_down"].rearrange("(f p) n -> p f n", p=P)[:, bass.ds(i * 2, 2), :])\
                    .then_inc(S["d_in"], 16)

            load("g", 0, True)
            load("u", 0, True)
            sp.dma_start(ident[:], io["ident"]).then_inc(S["const"], 16)
            sp.dma_start(g[:], io["g_final"].partition_broadcast(P)).then_inc(S["const"], 16)
            sp.dma_start(rows[0:taps, :], io["state_ffn_conv"]).then_inc(S["rows"], 16)
            sp.dma_start(rows[taps:taps + CONV_W, :], io["conv_w"]).then_inc(S["rows"], 16)
            sp.dma_start(rows[taps + CONV_W:COEF, :], io["conv_b"]).then_inc(S["rows"], 16)

            def body(i, start=False):
                load("g", i * 2 + 1)
                load("u", i * 2 + 1)
                load_d(i, start)
                load("g", i * 2 + 2)
                load("u", i * 2 + 2)

            def end(i):
                load("g", i * 2 + 1)
                load("u", i * 2 + 1)
                load_d(i)

            def tail(i):
                for t in range(NT):
                    sp.wait_ge(S["y_ok"], t + 1)
                    dst, n = (io["y_prompt"][t * P:(t + 1) * P, :], P) if t < PT else (io["y_sample"], NS)
                    sp.dma_start(dst, (gc, sg)[t % 2][0:n, 0:D_MODEL]).then_inc(S[f"out{t % 2}"], 16)
                sp.wait_ge(S["last_ev"], (FC + 3) // 4)
                sp.dma_start(io["p_ffn_conv"], rows[0:CONV_W - 1, :]).then_inc(S["out"], 16)
                sp.dma_start(io["s_ffn_conv"], rows[CONV_W - 1:LASTS, :]).then_inc(S["out"], 16)
                for n, k in (("out", 2), ("out0", (NT + 1) // 2), ("out1", NT // 2)):
                    sp.wait_ge(S[n], 16 * k)
                sp.wait_ge(io["moved"], io["moves"])

            sweep(sp, lambda i: body(i, True), body, end, tail)

        @block.gpsimd
        def _(pool):
            nc.gpsimd.memset(half, -0.5).then_inc(S["c_half"], 1)
            nc.gpsimd.memset(eps, EPS).then_inc(S["c_half"], 1)
            for c in range(2):
                for a in (a_hi, a_lo):
                    nc.gpsimd.memset(a[:, c, TOK:PAD].bitcast(F32), 0.0).then_inc(S["pad"], 1)

            def split(n, f):
                pool.wait_ge(S[n + "_hi"], f + 1)
                nc.gpsimd.tensor_tensor(w_lo[n][:], w_raw[n][:], w_hi[n][:].bitcast(F32), ALU.subtract)\
                    .then_inc(S[n + "_lo"], 1)

            def split_d(i):
                pool.wait_ge(S["d_hi"], i + 1)
                nc.gpsimd.tensor_tensor(d_lo[:], d_raw[:], d_hi[:].bitcast(F32), ALU.subtract).then_inc(S["d_lo"], 1)

            def body(i):
                split("g", i * 2 + 1)
                split("u", i * 2 + 1)
                split_d(i)
                split("g", i * 2 + 2)
                split("u", i * 2 + 2)

            def first(i):
                split("g", 0)
                split("u", 0)
                body(0)

            def end(i):
                split("g", i * 2 + 1)
                split("u", i * 2 + 1)
                split_d(i)

            def tail(i):
                for t in range(NT):
                    pool.wait_ge(S["ms"], t + 1)
                    nc.gpsimd.tensor_tensor(ms[t], ms[t], eps, ALU.add).then_inc(S["eps"], 1)
                    pool.wait_ge(S["eps"], t + 1)
                    nc.gpsimd.tensor_tensor(rs[t], ms[t], half, ALU.pow).then_inc(S["rs"], 1)

            sweep(pool, first, body, end, tail)

        @block.scalar
        def _(act):
            def high(n, f):
                act.wait_ge(S[n + "_in"], f * 16 + 16)
                nc.scalar.copy(w_hi[n][:], w_raw[n][:]).then_inc(S[n + "_hi"], 1)

            def chunk(i, c, more, down):
                f = i * 2 + c
                start = isinstance(i, int) and i == 0 and c == 0
                k = coef[:, bass.ds(f, 1), :].rearrange("p a n -> p (a n)")
                w2, b = k[:, taps + CONV_W - 1:taps + CONV_W], k[:, COEF - 1:COEF]
                act.wait_ge(S["g_ps"], f + 1)
                if not start:
                    act.wait_ge(S["silu"], f)
                    act.wait_ge(S["conv_s"], f)
                nc.scalar.activation(gc[:, 0:MAIN], gp[:, 0:MAIN], ACT.Identity, scale=w2, bias=b).then_inc(S["sink"], 1)
                nc.scalar.activation(gc[:, MAIN:TOK], gsp[:, 0:REST], ACT.Identity, scale=w2, bias=b)\
                    .then_inc(S["sink"], 1)
                gs = gsp[:, SAMPLE:REST]
                nc.scalar.copy(gx[:, :, CONV_W - 1:], gs.rearrange("p (b t) -> p b t", b=DEC_B)).then_inc(S["sink"], 1)
                nc.scalar.copy(gx[:, :, 0:CONV_W - 1], k[:, 0:taps].rearrange("p (b t) -> p b t", b=DEC_B)).then_inc(S["sink"], 1)
                l = lasts[:, bass.ds(f, 1), :].rearrange("p a n -> p (a n)")
                nc.scalar.copy(l[:, 0:CONV_W - 1], gsp[:, SAMPLE - CONV_W + 1:SAMPLE]).then_inc(S["sink"], 1)
                nc.scalar.copy(l[:, CONV_W - 1:].rearrange("p (b t) -> p b t", b=DEC_B),
                               gs.rearrange("p (b t) -> p b t", b=DEC_B)[:, :, DEC_T - CONV_W + 1:]).then_inc(S["copied"], 1)
                if more:
                    high("g", f + 1)
                act.wait_ge(S["conv"], f + 1)
                act.wait_ge(S["conv_s"], f + 1)
                if not start:
                    act.wait_ge(S["a_lo"], f)
                nc.scalar.activation(sg[:], gc[:], ACT.Silu).then_inc(S["silu"], 1)
                if more:
                    act.wait_ge(S["u_ps"], f + 1)
                    high("u", f + 1)
                act.wait_ge(S["mul"], f + 1)
                if down:
                    act.wait_ge(S["d_ps"], i * DT)
                nc.scalar.copy(a_hi[:, c, 0:TOK], sg[:]).then_inc(S["a_hi"], 1)
                if c == 0:
                    act.wait_ge(S["d_in"], i * 16 + 16)
                    nc.scalar.copy(d_hi[:], d_raw[:]).then_inc(S["d_hi"], 1)

            def first(i):
                high("g", 0)
                high("u", 0)
                act.wait_ge(S["coef_ps"], 1)
                nc.scalar.copy(coef[:].rearrange("p f n -> p (f n)"), usp[:, 0:FC * COEF]).then_inc(S["coef"], 1)
                act.wait_ge(S["coef"], 1)
                chunk(0, 0, True, False)
                chunk(0, 1, True, False)

            def body(i):
                chunk(i, 0, True, True)
                chunk(i, 1, True, False)

            def end(i):
                chunk(i, 0, True, True)
                chunk(i, 1, False, False)

            def tail(i):
                for t in range(NT):
                    act.wait_ge(S["d_add"], i * DT - DT + 2 * t + 2)
                    if t >= 2:
                        act.wait_ge(S[f"out{t % 2}"], 16 * (t // 2))
                    nc.scalar.activation((gc, sg)[t % 2][:, 0:D_MODEL], acc[:, t, :], ACT.Square, scale=D_MODEL ** -0.5,
                                         accum_out=ms[t]).then_inc(S["ms"], 1)
                for q in range((FC + 3) // 4):
                    n = min(4, FC - 4 * q)
                    act.wait_ge(S["last_ps"], q + 1)
                    src = (gp, gp, up, up)[q % 4][:, (q % 2) * 512:(q % 2) * 512 + n * P]
                    last = nc.scalar.copy(rows[0:LASTS, q * 512:q * 512 + n * P], src[0:LASTS])
                    last.then_inc(S["last_ev"], 1)

            sweep(act, first, body, end, tail)

        @block.vector
        def _(dve):
            def adds(i):
                for t in range(NT):
                    for h in range(2):
                        n = i * DT + (2 * t + h - DT + 1)
                        dve.wait_ge(S["d_ps"], n)
                        a = acc[:, t, h * 512:(h + 1) * 512]
                        nc.vector.tensor_tensor(a, dp[h][:], a, ALU.add).then_inc(S["d_add"], 1)
                    yield t

            def chunk(i, c, down):
                f = i * 2 + c
                start = isinstance(i, int) and i == 0 and c == 0
                k = coef[:, bass.ds(f, 1), :].rearrange("p a n -> p (a n)")
                w0, w1 = k[:, taps:taps + 1], k[:, taps + 1:taps + 2]
                dve.wait_ge(S["copied"], f + 1)
                for w, d, s in ((w1, 1, "tap1"), (w0, 2, "conv")):
                    if s == "conv":
                        dve.wait_ge(S["tap1"], f + 1)
                    for src, at, n, done in ((gp, d, MAIN, "sink"), (gsp, MAIN + d, SAMPLE - d, s)):
                        y = gc[:, at:at + n]
                        nc.vector.scalar_tensor_tensor(out=y, in0=src[:, 0:n], scalar=w, in1=y, op0=ALU.mult,
                                                       op1=ALU.add).then_inc(S[done], 1)
                gcs = gc[:, SEQ:TOK].rearrange("p (b t) -> p b t", b=DEC_B)
                for w, d, s in ((w1, 1, "conv_s1"), (w0, 2, "conv_s")):
                    if s == "conv_s":
                        dve.wait_ge(S["conv_s1"], f + 1)
                    nc.vector.scalar_tensor_tensor(out=gcs, in0=gx[:, :, CONV_W - 1 - d:CONV_W - 1 - d + DEC_T], scalar=w,
                                                   in1=gcs, op0=ALU.mult, op1=ALU.add).then_inc(S[s], 1)
                if down:
                    for _ in adds(i):
                        pass
                dve.wait_ge(S["silu"], f + 1)
                dve.wait_ge(S["u_ps"], f + 1)
                nc.vector.tensor_tensor(sg[:, MAIN:TOK], usp[:, 0:REST], sg[:, MAIN:TOK], ALU.mult)\
                    .then_inc(S["mul_s"], 1)
                nc.vector.tensor_tensor(sg[:, 0:MAIN], up[:, 0:MAIN], sg[:, 0:MAIN], ALU.mult).then_inc(S["mul"], 1)
                dve.wait_ge(S["a_hi"], f + 1)
                nc.vector.tensor_tensor(a_lo[:, c, 0:TOK], sg[:], a_hi[:, c, 0:TOK].bitcast(F32), ALU.subtract)\
                    .then_inc(S["a_lo"], 1)

            def pair(down):
                def run(i):
                    chunk(i, 0, down)
                    chunk(i, 1, False)
                return run

            def tail(i):
                def last(t):
                    dve.wait_ge(S["rs"], t + 1)
                    nc.vector.scalar_tensor_tensor(out=(gc, sg)[t % 2][:, 0:D_MODEL], in0=acc[:, t, :], scalar=rs[t],
                                                   in1=g[:], op0=ALU.mult, op1=ALU.mult).then_inc(S["y_ok"], 1)
                for t in adds(i):
                    if t:
                        last(t - 1)
                last(NT - 1)

            dve.wait_ge(S["const"], 32)
            sweep(dve, pair(False), pair(True), pair(True), tail)

        @block.tensor
        def _(pe):
            def product(n, f):
                out, outs, free, done = {"g": (gp, gsp, "conv", "g_ps"), "u": (up, usp, "mul", "u_ps")}[n]
                pe.wait_ge(S[n + "_lo"], f + 1)
                if not (isinstance(f, int) and f == 0):
                    pe.wait_ge(S[free], f)
                    if n == "g":
                        pe.wait_ge(S["copied"], f)
                for k in range(KC):
                    for i, (w, x) in enumerate(((w_hi, hT_h), (w_hi, hT_l), (w_lo, hT_h))):
                        s, e = k == 0 and i == 0, k == KC - 1 and i == 2
                        for c0, c1 in ((0, 512), (512, MAIN)):
                            nc.tensor.matmul(out[:, c0:c1], w[n][:, k, :], x[:, k, c0:c1], start=s, stop=e)
                        last = nc.tensor.matmul(outs[:, 0:REST], w[n][:, k, :], x[:, k, MAIN:TOK], start=s, stop=e)
                last.then_inc(S[done], 1)

            def down(i):
                pe.wait_ge(S["a_lo"], i * 2)
                pe.wait_ge(S["d_lo"], i)
                for t in range(NT):
                    for h in range(2):
                        n = i * DT + (2 * t + h - DT - 1)
                        if not (isinstance(i, int) and i == 1 and t == 0):
                            pe.wait_ge(S["d_add"], n)
                        for c in range(2):
                            for j, (a, w) in enumerate(((a_hi, d_hi), (a_hi, d_lo), (a_lo, d_hi))):
                                last = nc.tensor.matmul(dp[h][:], a[:, c, t * P:(t + 1) * P],
                                                        w[:, c, h * 512:(h + 1) * 512], start=(c == 0 and j == 0),
                                                        stop=(c == 1 and j == 2))
                        last.then_inc(S["d_ps"], 1)

            def first(i):
                pe.wait_ge(S["const"], 32)
                pe.wait_ge(S["rows"], 48)
                pe.wait_ge(S["pad"], 4)
                for f in range(FC):
                    last = nc.tensor.transpose(usp[:, f * COEF:(f + 1) * COEF], rows[:, f * P:(f + 1) * P],
                                               ident[0:COEF, 0:COEF])
                last.then_inc(S["coef_ps"], 1)
                product("g", 0)
                pe.wait_ge(S["coef"], 1)
                product("u", 0)
                product("g", 1)
                product("u", 1)

            def body(i):
                product("g", i * 2)
                product("u", i * 2)
                down(i)
                product("g", i * 2 + 1)
                product("u", i * 2 + 1)

            def tail(i):
                down(i)
                for q in range((FC + 3) // 4):
                    n = min(4, FC - 4 * q)
                    if q >= 4:
                        pe.wait_ge(S["last_ev"], q - 3)
                    for j in range(n):
                        dst = (gp, gp, up, up)[q % 4][0:LASTS, (q % 2) * 512 + j * P:(q % 2) * 512 + (j + 1) * P]
                        last = nc.tensor.transpose(dst, lasts[:, 4 * q + j, :], ident[:])
                    last.then_inc(S["last_ps"], 1)

            first(0)
            body(1)
            with pe.Fori(2, ITER) as i:
                body(i)
            tail(ITER)


PHASES = (project, prompt_attention, sample_latent_attention, sample_window_attention,
          output_projection, gated_mlp)


def hybrid_decoder_step(nc, io):
    with ExitStack() as ctx:
        io = {**io, "moved": ctx.enter_context(nc.semaphore("moved")), "moves": 16 * 2 * DEC_B}
        for phase in PHASES:
            if phase is output_projection:
                io["acc"] = ctx.enter_context(nc.sbuf_tensor("acc", [P, NT, D_MODEL], F32))
                for n in ("hT_h", "hT_l"):
                    io[n] = ctx.enter_context(nc.sbuf_tensor(n, [P, KC, TOK], F32R))
            with ExitStack() as own:
                used = []

                def sem(name):
                    used.append(own.enter_context(nc.semaphore(name)))
                    return used[-1]

                phase(nc, sem, io)
                for s in used:
                    nc.gpsimd.sem_clear(s)
                nc.all_engine_barrier()




_OUTS = [
    ("y_prompt", (1, SEQ, D_MODEL)), ("y_sample", (DEC_B, DEC_T, D_MODEL)),
    ("p_kv_latent", (1, 1, SEQ, KV_RANK)), ("p_k_rope", (1, 1, SEQ, ROPE)),
    ("p_win_k", (1, 1, SEQ, HEADS, HD)), ("p_win_v", (1, 1, SEQ, HEADS, HD)),
    ("p_ffn_conv", (1, 1, CONV_W - 1, D_FF)),
    ("s_kv_latent", (1, DEC_B, DEC_T, KV_RANK)), ("s_k_rope", (1, DEC_B, DEC_T, ROPE)),
    ("s_win_k", (1, DEC_B, PAST, HEADS, HD)), ("s_win_v", (1, DEC_B, PAST, HEADS, HD)),
    ("s_ffn_conv", (1, DEC_B, CONV_W - 1, D_FF)),
]
_VIEWS = {
    "x_prompt": "a s d -> (a s) d", "x_sample": "b t d -> (b t) d",
    "cache_kv_latent": "a n p c -> (a n) p c", "cache_k_rope": "a n p c -> (a n) p c",
    "state_win_k": "a b s h d -> (a b) s (h d)", "state_win_v": "a b s h d -> (a b) s (h d)",
    "state_ffn_conv": "a b j f -> (a b j) f", "page_table": "b n -> (b n)",
    "g_attn": "a d -> (a d)", "w_in": "a k n -> (a k) n", "g_q_a": "a d -> (a d)", "w_q_b": "a k n -> (a k) n",
    "g_kv_a": "a d -> (a d)", "w_uk": "a k n -> (a k) n", "w_uv": "a k n -> (a k) n", "w_out": "a k n -> (a k) n",
    "g_ffn": "a d -> (a d)", "w_gate": "a k n -> (a k) n", "w_up": "a k n -> (a k) n", "conv_w": "a j f -> (a j) f",
    "conv_b": "a f -> a f", "w_down": "a k n -> (a k) n", "g_final": "d -> d",
    "y_prompt": "a s d -> (a s) d", "y_sample": "b t d -> (b t) d",
    "p_kv_latent": "a b s c -> (a b s) c", "p_k_rope": "a b s c -> (a b s) c",
    "p_win_k": "a b s h d -> (a b s) (h d)", "p_win_v": "a b s h d -> (a b s) (h d)",
    "p_ffn_conv": "a b j f -> (a b j) f",
    "s_kv_latent": "a b s c -> (a b s) c", "s_k_rope": "a b s c -> (a b s) c",
    "s_win_k": "a b s h d -> (a b) s (h d)", "s_win_v": "a b s h d -> (a b) s (h d)",
    "s_ffn_conv": "a b j f -> (a b j) f",
}
_SCRATCH = {
    "s_dq": (TOK, HW), "s_q": (TOK, HEADS * QK), "s_k": (SEQ, HEADS * QK), "s_v": (SEQ, HW),
    "s_o": (KC, P, TOK),
}


def kernel(**inputs):
    import numpy as _np
    import concourse.bacc as _bacc
    from concourse import mybir as _mybir
    from concourse.bass_utils import run_bass_kernel_spmd as _run

    nc = _bacc.Bacc("TRN2", target_bir_lowering=False, num_devices=1)
    arrays, io = {}, {}
    for name, a in {**inputs, **shape_tables()}.items():
        a = _np.ascontiguousarray(a)
        arrays[f"in_{name}"] = a
        ap = nc.dram_tensor(f"in_{name}", a.shape, _mybir.dt.from_np(a.dtype), kind="ExternalInput").ap()
        io[name] = ap.rearrange(_VIEWS[name]) if name in _VIEWS else ap
    for name, shape in _OUTS:
        ap = nc.dram_tensor(f"out_{name}", shape, F32, kind="ExternalOutput").ap()
        io[name] = ap.rearrange(_VIEWS[name])
    for name, shape in _SCRATCH.items():
        io[name] = nc.dram_tensor(f"scratch_{name}", shape, F32, kind="Internal").ap()
    hybrid_decoder_step(nc, io)
    r = _run(nc, [arrays], core_ids=[0])
    return tuple(r.results[0][f"out_{name}"] for name, _ in _OUTS)
```
